# Optimizing a Trainium2 kernel written in Bass

```python
import math
import jax, jax.numpy as jnp
from jax import lax
import numpy as np

D_MODEL = 1024
BATCH = 1
SEQ = 1024
DEPTH = 1

N_META = 16
CHUNK = 64
GDN_HEADS = 8
GDN_DK = 128
GDN_DV = 128
GDN_CONV = 4
RET_HEADS = 4
RET_DK = 256
RET_DV = 256
D_FF = 2816
FFN_CONV = 3
ROPE_BASE = 10000.0
EPS = 1e-6

GDN_QK = GDN_HEADS * GDN_DK
GDN_V = GDN_HEADS * GDN_DV
RET_QK = RET_HEADS * RET_DK
RET_V = RET_HEADS * RET_DV
IN_WIDTHS = (GDN_QK, GDN_QK, GDN_V, GDN_V, GDN_HEADS, GDN_HEADS,
             RET_QK, RET_QK, RET_V, RET_V, D_MODEL, D_MODEL)
D_IN = sum(IN_WIDTHS)
SPLIT_IDX = tuple(int(i) for i in np.cumsum(IN_WIDTHS)[:-1])

kernel_name = 'hybrid_gdn_retention_convffn_meta'

def rmsnorm(x, g):
    xf = x.astype(jnp.float32)
    y = xf * lax.rsqrt(jnp.mean(xf * xf, axis=-1, keepdims=True) + EPS)
    return (y * g.astype(jnp.float32)).astype(x.dtype)

def causal_dwconv(x, w):
    K, C = w.shape
    return lax.conv_general_dilated(
        x, w[:, None, :].astype(x.dtype), window_strides=(1,), padding=[(K - 1, 0)],
        dimension_numbers=('NWC', 'WIO', 'NWC'), feature_group_count=C)

def l2norm(x):
    return x * lax.rsqrt(jnp.sum(x * x, axis=-1, keepdims=True) + EPS)

def rotary(x, pos):
    half = x.shape[-1] // 2
    inv = 1.0 / (ROPE_BASE ** (jnp.arange(half, dtype=jnp.float32) / half))
    ang = pos[:, None] * inv[None, :]
    cos = jnp.cos(ang)[None, :, None, :]
    sin = jnp.sin(ang)[None, :, None, :]
    x1, x2 = x[..., :half], x[..., half:]
    return jnp.concatenate([x1 * cos - x2 * sin, x2 * cos + x1 * sin], axis=-1)

def to_chunks(t, pad):
    widths = [(0, 0), (pad, 0)] + [(0, 0)] * (t.ndim - 2)
    t = jnp.pad(t, widths)
    B, Lp = t.shape[0], t.shape[1]
    t = t.reshape((B, Lp // CHUNK, CHUNK) + t.shape[2:])
    perm = (0, 3, 1, 2) + tuple(range(4, t.ndim))
    return t.transpose(perm)

def from_chunks(o, pad):
    N, B, H, C, d = o.shape
    o = o.transpose(1, 0, 3, 2, 4).reshape(B, N * C, H, d)
    return o[:, pad:]

def gated_delta_chunked(q, k, v, log_g, beta):
    L = q.shape[1]
    pad = (-L) % CHUNK
    dk = q.shape[-1]
    q = to_chunks(q * (dk ** -0.5), pad)
    k = to_chunks(k, pad)
    v = to_chunks(v, pad)
    beta = to_chunks(beta, pad)
    G = jnp.cumsum(to_chunks(log_g, pad), axis=-1)
    tril = jnp.asarray(np.tril(np.ones((CHUNK, CHUNK), dtype=bool)))
    strict = jnp.asarray(np.tril(np.ones((CHUNK, CHUNK), dtype=bool), -1))
    diff = G[..., :, None] - G[..., None, :]
    decay = jnp.where(tril, jnp.exp(jnp.where(tril, diff, 0.0)), 0.0)
    kb = k * beta[..., None]
    M = jnp.where(strict, jnp.einsum('bhncd,bhnsd->bhncs', kb, k) * decay, 0.0)
    eye = jnp.eye(CHUNK, dtype=M.dtype)
    T = lax.linalg.triangular_solve(eye + M, jnp.broadcast_to(eye, M.shape),
                                    left_side=True, lower=True, unit_diagonal=True)
    u = jnp.einsum('bhncs,bhnsd->bhncd', T, v * beta[..., None])
    w = jnp.einsum('bhncs,bhnsd->bhncd', T, kb * jnp.exp(G)[..., None])
    attn = jnp.einsum('bhncd,bhnsd->bhncs', q, k) * decay
    q_dec = q * jnp.exp(G)[..., None]
    G_last = G[..., -1]
    k_dec = k * jnp.exp(G_last[..., None] - G)[..., None]
    g_last = jnp.exp(G_last)

    def step(S, xs):
        u_c, w_c, a_c, qd_c, kd_c, gl_c = xs
        v_new = u_c - jnp.einsum('bhcd,bhde->bhce', w_c, S)
        o_c = jnp.einsum('bhcd,bhde->bhce', qd_c, S) + jnp.einsum('bhcs,bhse->bhce', a_c, v_new)
        S = S * gl_c[..., None, None] + jnp.einsum('bhcd,bhce->bhde', kd_c, v_new)
        return S, o_c

    xs = tuple(jnp.moveaxis(t, 2, 0) for t in (u, w, attn, q_dec, k_dec, g_last))
    B, H = q.shape[0], q.shape[1]
    S0 = jnp.zeros((B, H, dk, v.shape[-1]), jnp.float32)
    _, o = lax.scan(step, S0, xs)
    return from_chunks(o, pad)

def retention_chunked(q, k, v):
    H = q.shape[2]
    dk = q.shape[-1]
    lg = jnp.log(1.0 - 2.0 ** (-5.0 - jnp.arange(H, dtype=jnp.float32)))
    L = q.shape[1]
    pad = (-L) % CHUNK
    q = to_chunks(q, pad)
    k = to_chunks(k * (dk ** -0.5), pad)
    v = to_chunks(v, pad)
    idx = jnp.arange(CHUNK, dtype=jnp.float32)
    tril = jnp.asarray(np.tril(np.ones((CHUNK, CHUNK), dtype=bool)))
    dmask = jnp.where(tril, jnp.exp((idx[:, None] - idx[None, :]) * lg[:, None, None]), 0.0)
    inner = jnp.einsum('bhncs,bhnse->bhnce',
                       jnp.einsum('bhncd,bhnsd->bhncs', q, k) * dmask[None, :, None], v)
    q_dec = q * jnp.exp((idx[None, :] + 1.0) * lg[:, None])[None, :, None, :, None]
    k_dec = k * jnp.exp((CHUNK - 1.0 - idx[None, :]) * lg[:, None])[None, :, None, :, None]
    g_chunk = jnp.exp(CHUNK * lg)[None, :, None, None]

    def step(S, xs):
        in_c, qd_c, kd_c, v_c = xs
        o_c = in_c + jnp.einsum('bhcd,bhde->bhce', qd_c, S)
        S = S * g_chunk + jnp.einsum('bhcd,bhce->bhde', kd_c, v_c)
        return S, o_c

    xs = tuple(jnp.moveaxis(t, 2, 0) for t in (inner, q_dec, k_dec, v))
    S0 = jnp.zeros((q.shape[0], H, dk, v.shape[-1]), jnp.float32)
    _, o = lax.scan(step, S0, xs)
    return from_chunks(o, pad)

def mixer_block(hn, pos, w_in, conv_w, a_log, dt_bias, gdn_norm, w_out):
    B, L, _ = hn.shape
    f32 = jnp.float32
    proj = hn @ w_in.astype(hn.dtype)
    gq, gk, gv, gz, ga, gb, rq, rk, rv, rg, gate_a, gate_b = jnp.split(proj, SPLIT_IDX, axis=-1)
    qkv = jax.nn.silu(causal_dwconv(jnp.concatenate([gq, gk, gv], axis=-1), conv_w))
    gq, gk, gv = jnp.split(qkv.astype(f32), (GDN_QK, 2 * GDN_QK), axis=-1)
    gq = l2norm(gq.reshape(B, L, GDN_HEADS, GDN_DK))
    gk = l2norm(gk.reshape(B, L, GDN_HEADS, GDN_DK))
    gv = gv.reshape(B, L, GDN_HEADS, GDN_DV)
    beta = jax.nn.sigmoid(gb.astype(f32))
    log_g = -jnp.exp(a_log.astype(f32)) * jax.nn.softplus(ga.astype(f32) + dt_bias.astype(f32))
    o_a = gated_delta_chunked(gq, gk, gv, log_g, beta)
    o_a = o_a * lax.rsqrt(jnp.mean(o_a * o_a, axis=-1, keepdims=True) + EPS) * gdn_norm.astype(f32)
    y_a = (o_a * jax.nn.silu(gz.astype(f32).reshape(B, L, GDN_HEADS, GDN_DV))).reshape(B, L, GDN_V)
    rq = rotary(rq.astype(f32).reshape(B, L, RET_HEADS, RET_DK), pos)
    rk = rotary(rk.astype(f32).reshape(B, L, RET_HEADS, RET_DK), pos)
    o_b = retention_chunked(rq, rk, rv.astype(f32).reshape(B, L, RET_HEADS, RET_DV))
    o_b = o_b * lax.rsqrt(jnp.mean(o_b * o_b, axis=-1, keepdims=True) + EPS)
    y_b = jax.nn.silu(rg.astype(f32)) * o_b.reshape(B, L, RET_V)
    y = jax.nn.sigmoid(gate_a.astype(f32)) * y_a + jax.nn.sigmoid(gate_b.astype(f32)) * y_b
    return y.astype(hn.dtype) @ w_out.astype(hn.dtype)

def conv_ffn(hn, w_up, conv_w, conv_b, w_down):
    u = causal_dwconv(hn @ w_up.astype(hn.dtype), conv_w) + conv_b.astype(hn.dtype)
    a, b = jnp.split(u, 2, axis=-1)
    return (jax.nn.silu(a) * b) @ w_down.astype(hn.dtype)

def setup_inputs(seed: int = 0) -> dict:
    key = jax.random.key(seed)
    ks = jax.random.split(key, 16)
    f32 = jnp.float32
    nrm = lambda k, shape, s: jax.random.normal(k, shape, f32) * s
    dt = jnp.exp(jax.random.uniform(ks[6], (DEPTH, GDN_HEADS), f32, math.log(1e-3), math.log(1e-1)))
    return {
        'x': nrm(ks[0], (BATCH, SEQ, D_MODEL), 1.0),
        'meta': nrm(ks[1], (N_META, D_MODEL), 1.0),
        'norm1': 1.0 + nrm(ks[2], (DEPTH, D_MODEL), 0.02),
        'w_in': nrm(ks[3], (DEPTH, D_MODEL, D_IN), D_MODEL ** -0.5),
        'gdn_conv_w': nrm(ks[4], (DEPTH, GDN_CONV, 2 * GDN_QK + GDN_V), GDN_CONV ** -0.5),
        'gdn_a_log': jnp.log(jax.random.uniform(ks[5], (DEPTH, GDN_HEADS), f32, 1.0, 16.0)),
        'gdn_dt_bias': dt + jnp.log(-jnp.expm1(-dt)),
        'gdn_norm': 1.0 + nrm(ks[7], (DEPTH, GDN_DV), 0.02),
        'w_out': nrm(ks[8], (DEPTH, D_MODEL, D_MODEL), D_MODEL ** -0.5),
        'norm2': 1.0 + nrm(ks[9], (DEPTH, D_MODEL), 0.02),
        'w_ffn_up': nrm(ks[10], (DEPTH, D_MODEL, 2 * D_FF), D_MODEL ** -0.5),
        'ffn_conv_w': nrm(ks[11], (DEPTH, FFN_CONV, 2 * D_FF), FFN_CONV ** -0.5),
        'ffn_conv_b': nrm(ks[12], (DEPTH, 2 * D_FF), 0.02),
        'w_ffn_down': nrm(ks[13], (DEPTH, D_FF, D_MODEL), D_FF ** -0.5),
        'norm_f': 1.0 + nrm(ks[14], (D_MODEL,), 0.02),
    }

def reference(x, meta, norm1, w_in, gdn_conv_w, gdn_a_log, gdn_dt_bias, gdn_norm, w_out,
              norm2, w_ffn_up, ffn_conv_w, ffn_conv_b, w_ffn_down, norm_f):
    B = x.shape[0]
    h = jnp.concatenate(
        [jnp.broadcast_to(meta.astype(x.dtype)[None], (B, N_META, D_MODEL)), x], axis=1)
    pos = jnp.arange(h.shape[1], dtype=jnp.float32)
    for layer in range(DEPTH):
        h = h + mixer_block(rmsnorm(h, norm1[layer]), pos, w_in[layer], gdn_conv_w[layer],
                            gdn_a_log[layer], gdn_dt_bias[layer], gdn_norm[layer], w_out[layer])
        h = h + conv_ffn(rmsnorm(h, norm2[layer]), w_ffn_up[layer], ffn_conv_w[layer],
                         ffn_conv_b[layer], w_ffn_down[layer])
    h = rmsnorm(h, norm_f)
    return h[:, N_META:]


_drawn_inputs = setup_inputs


def setup_inputs(seed=0):
    import zlib

    import numpy as np

    out = dict(_drawn_inputs(seed))
    spreads = {}
    factors = {'norm1': 3.116, 'gdn_norm': 8.0, 'norm2': 10.973, 'ffn_conv_b': 22.117, 'norm_f': 23.601}
    for name, (base, spread) in spreads.items():
        noise = np.random.default_rng([zlib.crc32(name.encode()), seed]).standard_normal(out[name].shape)
        drawn = base * np.exp(spread * noise) if base else spread * noise
        out[name] = __import__('jax').numpy.asarray(drawn.astype(out[name].dtype))
    for name, factor in factors.items():
        out[name] = (out[name] * factor).astype(out[name].dtype)
    return out
```

```python
import math
from contextlib import ExitStack

import numpy as np

import concourse.bass as bass
from concourse import mybir

F32 = mybir.dt.float32
F32R = mybir.dt.float32r
ACT = mybir.ActivationFunctionType
ALU = mybir.AluOpType
AX = mybir.AxisListType

P = 128
D = 1024
KC = D // P
SEQ = 1024
META = 16
CH = 128
NCH = 9
T = NCH * CH
PAD = T - META - SEQ
GH = 8
RH = 4
HALF = 128
D_FF = 2816
FT = D_FF // P
GCONV = 4
FCONV = 3
EPS = 1e-6
SLOTS = 2

A_COL = PAD - 4
A_N = (T - A_COL) // 3
C_COL = PAD + META - (FCONV - 1)
C_W = T - C_COL
C_N = C_W // 3
X0 = PAD + META

Q0, K0, V0, Z0 = 0, 1024, 2048, 3072
GA0 = 4096
RQ0 = GA0 + 2 * GH
RK0, RV0, RG0, GATEA0, GATEB0 = (RQ0 + D * n for n in range(1, 6))

PAR_GCONV = 0
PAR_N1 = PAR_GCONV + GCONV * 24
PAR_N2 = PAR_N1 + KC
PAR_GN = PAR_N2 + KC
PAR_FCONV = PAR_GN + 1
PAR_FB = PAR_FCONV + FCONV * 2 * FT
PAR_W = PAR_FB + 2 * FT

C_ID = 0
C_ONES = C_ID + P
C_TRIU = C_ONES + P
C_UPTO = C_TRIU + P
C_BELOW = C_UPTO + P
C_LEVEL = C_BELOW + P
NLEVEL = 7
C_RDEC = C_LEVEL + NLEVEL * 64
C_RROW = C_RDEC + RH * CH
C_RCOL = C_RROW + RH * CH
C_EPS = C_RCOL + RH
C_LNQ = C_EPS + 1
C_W_ALL = C_LNQ + 1

S_Q, S_K, S_V = 0, 8, 16
S_ZA, S_ZB = 24, 32
S_RQ, S_RK, S_RV = 40, 48, 56
S_N = 64


def shape_constants():
    c = np.zeros((P, C_W_ALL), np.float64)
    i = np.arange(P)
    c[:, C_ID:C_ID + P] = np.eye(P)
    c[:, C_ONES:C_ONES + P] = 1
    upto = i[:, None] <= i[None, :]
    c[:, C_TRIU:C_TRIU + P] = upto
    c[:, C_UPTO:C_UPTO + P] = np.where(upto, 0, -1e30)
    c[:, C_BELOW:C_BELOW + P] = np.where(i[None, :] < i[:, None], 0, 1e30)
    for lv in range(NLEVEL):
        b = 1 << lv
        odd = np.array([m for m in range(P) if (m // b) % 2])
        c[:, C_LEVEL + 64 * lv:C_LEVEL + 64 * lv + 64] = -1.0 * (i[:, None] // b == odd[None, :] // b - 1)
    lg = np.log(1.0 - 2.0 ** (-5.0 - np.arange(RH)))
    scale = (2 * HALF) ** -0.5
    for h in range(RH):
        dec = np.where(upto, np.exp(np.minimum(i[None, :] - i[:, None], CH) * lg[h]), 0) * scale
        c[:, C_RDEC + CH * h:C_RDEC + CH * h + CH] = dec
        c[:, C_RROW + CH * h:C_RROW + CH * h + CH] = np.exp((i[None, :] + 1) * lg[h])
        c[:, C_RCOL + h] = np.exp((CH - 1 - i) * lg[h]) * scale
    c[:, C_EPS] = EPS
    c[:, C_LNQ] = math.log(P ** -0.5)
    half = HALF
    inv = (1.0 / (np.float32(10000.0) ** (np.arange(half, dtype=np.float32) / np.float32(half)))).astype(np.float32)
    pos = np.arange(META + SEQ, dtype=np.float32)
    ang = (pos[None, :] * inv[:, None]).astype(np.float32).astype(np.float64)
    rope = np.stack([np.cos(ang), np.sin(ang)], 1)
    return c.astype(np.float32), rope.astype(np.float32)


def project(pe, psum, bank, wh, wl, xh, xl, col, n, block_ready=None):
    for k in range(KC):
        if block_ready is not None:
            pe.wait_ge(block_ready, k + 1)
        for part, (w, x) in enumerate(((wh, xh), (wh, xl), (wl, xh))):
            for j in range(3):
                mm = pe.matmul(psum[:, bank + j, 0:n], w[:, k, :], x[:, k, col + n * j:col + n * j + n],
                               start=(k == 0 and part == 0), stop=(k == KC - 1 and part == 2))
    return mm


def input_phase(nc, io, sc):
    with ExitStack() as ctx:
        def sb(name, shape, dt=F32):
            return ctx.enter_context(nc.sbuf_tensor(name, shape, dt))

        def sem(name):
            return ctx.enter_context(nc.semaphore(name))

        psum = ctx.enter_context(nc.psum_tensor("a_psum", [P, 8, 512], F32))
        cst = sb("a_cst", [P, C_W_ALL])
        rope = sb("rope", [P, 2, META + SEQ])
        prow = sb("param_rows", [P, 3, P])
        par = sb("a_par", [P, PAR_W])
        arow = sb("decay_rows", [P, 2, GH])
        xt = sb("x_tokens", [P, SLOTS, D])
        hT = sb("hT", [P, KC, T])
        sq = sb("squares", [P, SLOTS, KC, CH])
        ssq = sb("square_sums", [P, T])
        rbc = sb("rms_rows", [P, T])
        xn = sb("normed_block", [P, SLOTS, T])
        xh = sb("xh", [P, KC, T], F32R)
        xl = sb("xl", [P, KC, T], F32R)
        wraw = [sb(f"w_raw{s}", [P, KC, P]) for s in range(SLOTS)]
        wh = [sb(f"w_hi{s}", [P, KC, P], F32R) for s in range(SLOTS)]
        wl = [sb(f"w_lo{s}", [P, KC, P], F32R) for s in range(SLOTS)]
        raw = [xt[:, 0:2, :].rearrange("p a b -> p (a b)")[:, 0:3 * A_N],
               sq[:, 0:2, :, :].rearrange("p a b c -> p (a b c)")[:, 0:3 * A_N]]
        work = [ssq[:, :], rbc[:, :]]
        stage = [xn[:, 0, :], xn[:, 1, :]]

        abT = sb("gates_T", [2 * GH, T])
        gates = sb("gates", [P, NCH, 2 * GH])
        gtmp = sb("gates_work", [P, NCH, 2 * GH])
        gabs = sb("gates_abs", [P, NCH, GH])
        rate = sb("decay_rate", [P, GH])
        AB_STEPS = 12

        consts_in = sem("consts_in")
        params_in = sem("params_in")
        x_in = [sem(f"x_in{s}") for s in range(SLOTS)]
        rope_in = sem("rope_in")
        pad_zero = sem("pad_zero")
        turned = sem("turned")
        par_out = sem("par_out")
        hT_out = sem("hT_out")
        squared = sem("squared")
        summed = sem("summed")
        ss_ready = sem("ss_ready")
        ln_done = sem("ln_done")
        rms_ready = sem("rms_ready")
        normed = sem("normed")
        x_hi = sem("x_hi")
        x_split = sem("x_split")
        h_stored = sem("h_stored")
        w_loaded = [sem(f"w_loaded{s}") for s in range(SLOTS)]
        w_hi = sem("w_hi")
        w_lo = sem("w_lo")
        mm_done = sem("mm_done")
        evac = sem("evac")
        taps = sem("taps")
        conv_done = sem("conv_done")
        activated = sem("activated")
        gate_mul = sem("gate_mul")
        gated = sem("gated")
        rot_mul = sem("rot_mul")
        rotated = sem("rotated")
        copied = sem("copied")
        stored = [sem(f"stored{s}") for s in range(SLOTS)]
        ab_raw = sem("ab_raw")
        ab_turned = sem("ab_turned")
        ab_step = sem("ab_step")
        ab_stored = sem("ab_stored")
        block = ctx.enter_context(nc.Block())

        w_in = io["w_in"][0].rearrange("(k p) n -> p k n", p=P)
        NT = 80
        CONV, ZA, ZB, ROT, RV = (
            (0, 12, Q0, 256, Q0 + P, 256),
            (12, 8, Z0, P, GATEA0, P),
            (20, 8, RG0, P, GATEB0, P),
            (28, 8, RQ0, 256, RQ0 + P, 256),
            (36, 4, RV0, 256, RV0 + P, 256))
        SEGMENTS = (CONV, ZA, ZB, ROT, RV)

        @block.sync
        def _(sp):
            sp.dma_start(cst[:, :], io["cst"]).then_inc(consts_in, 16)
            sp.dma_start(xt[PAD:P, 0, :], io["meta"]).then_inc(x_in[0], 16)
            sp.dma_start(xt[:, 1, :], io["x"][0, 0:P, :]).then_inc(x_in[1], 16)
            g = prow[0:96, 0, :]
            sp.dma_start(g, io["gdn_conv_w"][0].rearrange("j (t p) -> (j t) p", p=P)).then_inc(params_in, 16)
            sp.dma_start(prow[96:104, 0, :], io["norm1"][0].rearrange("(t p) -> t p", p=P)).then_inc(params_in, 16)
            sp.dma_start(prow[104:112, 0, :], io["norm2"][0].rearrange("(t p) -> t p", p=P)).then_inc(params_in, 16)
            sp.dma_start(prow[112:113, 0, :], io["gdn_norm"]).then_inc(params_in, 16)
            fw = io["ffn_conv_w"][0].rearrange("j (t p) -> j t p", p=P)
            fb = io["ffn_conv_b"][0].rearrange("(t p) -> t p", p=P)
            sp.dma_start(prow[0:44, 1, :], fw[0]).then_inc(params_in, 16)
            sp.dma_start(prow[44:88, 1, :], fw[1]).then_inc(params_in, 16)
            sp.dma_start(prow[0:44, 2, :], fw[2]).then_inc(params_in, 16)
            sp.dma_start(prow[44:88, 2, :], fb).then_inc(params_in, 16)
            sp.dma_start(arow[:, 0, :], io["gdn_a_log"].broadcast_to((P, GH))).then_inc(params_in, 16)
            sp.dma_start(arow[:, 1, :], io["gdn_dt_bias"].broadcast_to((P, GH))).then_inc(params_in, 16)
            for s in range(SLOTS):
                sp.dma_start(wraw[s][:, :, :], w_in[:, :, Q0 + P * s:Q0 + P * s + P]).then_inc(w_loaded[s], 16)
            for c in range(2, NCH):
                sp.wait_ge(turned, c - 1)
                sp.dma_start(xt[:, c % 2, :], io["x"][0, (c - 1) * P:c * P, :]).then_inc(x_in[c % 2], 16)
            sp.dma_start(rope[:, :, :], io["rope"]).then_inc(rope_in, 16)
            sp.wait_ge(hT_out, NCH)
            sp.dma_start(sc["hT"], hT[:, :, :]).then_inc(h_stored, 16)
            mix = sc["mix"].rearrange("s p c -> p s c")
            for s in range(SLOTS):
                sp.sem_inc(stored[s], 16)

            def load(pair, starts):
                for s in range(SLOTS):
                    sp.wait_ge(w_lo, pair * 2 + (s + 1))
                    sp.dma_start(wraw[s][:, :, :], w_in[:, :, bass.ds(starts[s], P)]).then_inc(w_loaded[s], 16)

            def store(s, tile, done, count):
                sp.wait_ge(done, count)
                sp.dma_start(mix[:, bass.ds(tile, 1), :],
                             stage[s].rearrange("p (o c) -> p o c", o=1)).then_inc(stored[s], 16)

            def store_pair(seg, i):
                if seg is CONV:
                    for s in range(SLOTS):
                        store(s, i * 2 + s, activated, i * 2 + (s + 3))
                elif seg is ZA or seg is ZB:
                    g = i + (seg[0] - ZA[0])
                    store(0, g + S_ZA, gated, g + 2)
                elif seg is ROT:
                    store(0, i * 2 + S_RQ, rot_mul, i * 5 + 3)
                    store(1, i * 2 + (S_RQ + 1), rotated, i + 2)
                else:
                    for s in range(SLOTS):
                        store(s, i * 2 + (S_RV + s), evac, i * 2 + (2 * RV[0] + s + 3))

            for n, seg in enumerate(SEGMENTS):
                first, pairs, a0, da, b0, db = seg
                with sp.Fori(0, pairs - 1) as i:
                    load(i + first, (i * da + (a0 + da), i * db + (b0 + db)))
                    store_pair(seg, i)
                if n + 1 < len(SEGMENTS):
                    load(first + pairs - 1, (SEGMENTS[n + 1][2], SEGMENTS[n + 1][4]))
                    store_pair(seg, pairs - 1)
            sp.wait_ge(w_lo, NT - 1)
            sp.dma_start(wraw[0][:, :, 0:2 * GH], w_in[:, :, GA0:GA0 + 2 * GH]).then_inc(w_loaded[0], 16)
            store_pair(RV, RV[1] - 1)
            for s in range(SLOTS):
                sp.wait_ge(stored[s], 16 * (41 - 16 * s))
            sp.wait_ge(h_stored, 16)
            sp.wait_ge(ab_step, AB_STEPS)
            sp.dma_start(sc["gates"], gates[:, :, :]).then_inc(ab_stored, 16)
            sp.dma_start(sc["par"], par[:, :]).then_inc(ab_stored, 16)
            sp.wait_ge(ab_stored, 32)

        @block.tensor
        def _(pe):
            pe.wait_ge(consts_in, 16)
            ident = cst[:, C_ID:C_ID + P]
            for c in range(NCH):
                s = c % 2
                pe.wait_ge(x_in[s], 16 * (c // 2 + 1))
                if c == 0:
                    pe.wait_ge(pad_zero, 1)
                if c >= 2:
                    pe.wait_ge(hT_out, c - 1)
                for k in range(KC):
                    mm = pe.transpose(psum[:, 2 * s + k // 4, (k % 4) * P:(k % 4) * P + P],
                                      xt[:, s, k * P:k * P + P], ident)
                mm.then_inc(turned, 1)
            pe.wait_ge(params_in, 160)
            for g, rows in enumerate((113, 88, 88)):
                mm = pe.transpose(psum[:, 7, g * P:g * P + rows], prow[0:rows, g, :], ident[0:rows, 0:rows])
            mm.then_inc(turned, 1)
            pe.wait_ge(summed, NCH)
            for j in range(3):
                mm = pe.matmul(psum[:, 4 + j, 0:T // 3], cst[:, C_ONES:C_ONES + P],
                               ssq[:, j * (T // 3):(j + 1) * (T // 3)], start=True, stop=True)
            mm.then_inc(ss_ready, 1)

            def tile(p, s, block_ready=None):
                pe.wait_ge(w_lo, p + 1)
                pe.wait_ge(evac, p + 1)
                project(pe, psum, 3 * s, wh[s], wl[s], xh, xl, A_COL, A_N, block_ready).then_inc(mm_done, 1)

            pe.wait_ge(rms_ready, 1)
            tile(0, 0, x_split)
            tile(1, 1)
            with pe.Fori(1, NT // 2) as i:
                for s in range(SLOTS):
                    tile(i * 2 + s, s)
            tile(NT, 0)
            pe.wait_ge(ab_raw, 2)
            for c in range(NCH):
                mm = pe.transpose(psum[:, 6, c * 2 * GH:(c + 1) * 2 * GH],
                                  abT[:, c * CH:c * CH + CH], ident[0:2 * GH, 0:2 * GH])
            mm.then_inc(ab_turned, 1)

        @block.scalar
        def _(act):
            act.sem_inc(evac, SLOTS)
            act.sem_inc(activated, SLOTS)
            act.preload_act_table_set("natural_log_exp_and_others")
            act.wait_ge(consts_in, 16)
            for c in range(NCH):
                s = c % 2
                act.wait_ge(turned, c + 1)
                act.activation(hT[:, :, c * CH:c * CH + CH], psum[:, 2 * s:2 * s + 2, :].rearrange(
                    "p b (k c) -> p (b k) c", c=CH), ACT.Copy).then_inc(hT_out, 1)
            for s in range(SLOTS):
                act.wait_ge(w_loaded[s], 16)
                act.activation(wh[s][:, :, :], wraw[s][:, :, :], ACT.Copy).then_inc(w_hi, 1)
            act.wait_ge(ss_ready, 1)
            act.activation(rbc[:, :].rearrange("p (b c) -> p b c", b=3), psum[:, 4:7, 0:T // 3], ACT.Ln,
                           bias=cst[:, C_EPS:C_EPS + 1], scale=1.0 / D).then_inc(ln_done, 1)
            act.wait_ge(ln_done, 1)
            act.activation(rbc[:, :], rbc[:, :], ACT.Exp, scale=-0.5).then_inc(rms_ready, 1)
            for k in range(KC):
                act.wait_ge(normed, k + 1)
                act.activation(xh[:, k, :], xn[:, k % 2, :], ACT.Copy).then_inc(x_hi, 1)

            def banks(s):
                return psum[:, 3 * s:3 * s + 3, 0:A_N]

            def flat(buf):
                return buf[:, 0:3 * A_N].rearrange("p (b c) -> p b c", b=3)

            def split_next(pair, s):
                act.wait_ge(w_loaded[s], pair * 16 + 32)
                act.activation(wh[s][:, :, :], wraw[s][:, :, :], ACT.Copy).then_inc(w_hi, 1)

            act.wait_ge(x_split, KC)
            act.preload_act_table_set("silu_and_others")
            with act.Fori(0, CONV[1]) as i:
                for s in range(SLOTS):
                    act.wait_ge(mm_done, i * 2 + s + 1)
                    act.wait_ge(conv_done, i * 2 + s + 1)
                    act.activation(flat(raw[s]), banks(s), ACT.Copy).then_inc(evac, 1)
                    split_next(i, s)
                    act.wait_ge(conv_done, i * 2 + s + 3)
                    act.wait_ge(stored[s], i * 16 + 16)
                    act.activation(stage[s][:, PAD:T], work[s][:, 0:T - PAD], ACT.Silu).then_inc(activated, 1)
            act.preload_act_table_set("sigmoid_and_others")
            act.wait_ge(activated, 24 + SLOTS)
            with act.Fori(0, ZA[1] + ZB[1]) as i:
                act.wait_ge(mm_done, i * 2 + (2 * ZA[0] + 1))
                act.wait_ge(gated, i + 1)
                act.activation(flat(raw[0]), banks(0), ACT.Copy)
                act.activation(flat(work[0]), banks(0), ACT.Sigmoid).then_inc(evac, 1)
                split_next(i + ZA[0], 0)
                act.wait_ge(mm_done, i * 2 + (2 * ZA[0] + 2))
                act.activation(flat(work[1]), banks(1), ACT.Sigmoid).then_inc(evac, 1)
                split_next(i + ZA[0], 1)
            act.wait_ge(gated, 17)
            with act.Fori(0, ROT[1]) as i:
                for s in range(SLOTS):
                    act.wait_ge(mm_done, i * 2 + (2 * ROT[0] + s + 1))
                    act.wait_ge(rotated, i + 1)
                    act.activation(flat(raw[s]), banks(s), ACT.Copy).then_inc(evac, 1)
                    split_next(i + ROT[0], s)

            def values(i, s, more):
                act.wait_ge(mm_done, i * 2 + (2 * RV[0] + s + 1))
                act.wait_ge(stored[s], i * 16 + 16 * (RV[0] - 16 * s + 1))
                act.activation(flat(stage[s][:, A_COL:T]), banks(s), ACT.Copy).then_inc(evac, 1)
                if more:
                    split_next(i + RV[0], s)

            act.wait_ge(rotated, 9)
            with act.Fori(0, RV[1] - 1) as i:
                for s in range(SLOTS):
                    values(i, s, True)
            values(RV[1] - 1, 0, True)
            values(RV[1] - 1, 1, False)
            act.preload_act_table_set("natural_log_exp_and_others")
            act.wait_ge(mm_done, NT + 1)
            act.activation(abT[:, A_COL:T].rearrange("p (b c) -> p b c", b=3), psum[0:2 * GH, 0:3, 0:A_N],
                           ACT.Copy).then_inc(ab_raw, 1)
            act.wait_ge(ab_step, 1)
            turned_gates = psum[:, 6, 0:NCH * 2 * GH].rearrange("p (c g) -> p c g", c=NCH)
            act.activation(gtmp[:, :, GH:2 * GH], turned_gates[:, :, GH:2 * GH], ACT.Exp,
                           scale=-1.0).then_inc(ab_step, 1)
            act.activation(gabs[:, :, :], gtmp[:, :, 0:GH], ACT.Abs).then_inc(ab_step, 1)
            act.wait_ge(ab_step, 3)
            act.activation(gabs[:, :, :], gabs[:, :, :], ACT.Exp, scale=-1.0).then_inc(ab_step, 1)
            act.wait_ge(ab_step, 4)
            act.activation(gabs[:, :, :], gabs[:, :, :], ACT.Ln, bias=1.0).then_inc(ab_step, 1)
            act.activation(rate[:, :], arow[:, 0, :], ACT.Exp).then_inc(ab_step, 1)

        @block.vector
        def _(dve):
            dve.sem_inc(conv_done, SLOTS)
            dve.sem_inc(gated, 1)
            dve.sem_inc(rotated, 1)
            dve.memset(xt[0:PAD, 0, :], 0.0).then_inc(pad_zero, 1)
            for c in range(NCH):
                dve.wait_ge(squared, c + 1)
                dve.tensor_reduce(ssq[:, c * CH:c * CH + CH], sq[:, c % 2, :, :].rearrange("p k c -> p c k"),
                                  AX.X, ALU.add).then_inc(summed, 1)
            dve.wait_ge(turned, NCH + 1)
            for g, (at, n) in enumerate(((0, PAR_FCONV), (PAR_FCONV, 88), (PAR_FCONV + 88, 88))):
                dve.tensor_copy(par[:, at:at + n], psum[:, 7, g * P:g * P + n]).then_inc(par_out, 1)
            for s in range(SLOTS):
                dve.wait_ge(w_hi, s + 1)
                dve.tensor_tensor(wl[s][:, :, :], wraw[s][:, :, :], wh[s][:, :, :].bitcast(F32),
                                  ALU.subtract).then_inc(w_lo, 1)
            dve.wait_ge(par_out, 3)
            dve.wait_ge(rms_ready, 1)

            def low_part(k):
                dve.wait_ge(normed, k + 1)
                dve.wait_ge(x_hi, k + 1)
                dve.tensor_tensor(xl[:, k, :], xn[:, k % 2, :], xh[:, k, :].bitcast(F32),
                                  ALU.subtract).then_inc(x_split, 1)

            for k in range(KC):
                if k >= 2:
                    dve.wait_ge(x_split, k - 1)
                dve.scalar_tensor_tensor(out=xn[:, k % 2, :], in0=hT[:, k, :], scalar=par[:, PAR_N1 + k:PAR_N1 + k + 1],
                                         in1=rbc[:, :], op0=ALU.mult, op1=ALU.mult).then_inc(normed, 1)
                if k:
                    low_part(k - 1)
            low_part(KC - 1)

            def split_low(tile, s):
                dve.wait_ge(w_hi, tile + 1)
                dve.tensor_tensor(wl[s][:, :, :], wraw[s][:, :, :], wh[s][:, :, :].bitcast(F32),
                                  ALU.subtract).then_inc(w_lo, 1)

            N = T - PAD
            with dve.Fori(0, CONV[1]) as i:
                for s in range(SLOTS):
                    p = i * 2 + s
                    acc = work[s][:, 0:N]
                    dve.wait_ge(evac, i * 2 + s + 3)
                    dve.wait_ge(activated, i * 2 + s + 1)

                    def tap(j):
                        return raw[s][:, 1 + j:1 + j + N], par[:, bass.ds(i * 2 + (s + PAR_GCONV + 24 * j), 1)]

                    x, w = tap(0)
                    dve.tensor_scalar(acc, x, w, None, ALU.mult).then_inc(taps, 1)
                    for j in range(1, GCONV):
                        x, w = tap(j)
                        dve.wait_ge(taps, i * 6 + (3 * s + j))
                        dve.scalar_tensor_tensor(out=acc, in0=x, scalar=w, in1=acc, op0=ALU.mult,
                                                 op1=ALU.add).then_inc(taps if j < 3 else conv_done, 1)
                    split_low(i * 2 + (s + 2), s)

            def gate(i, pair0, zout, norm):
                dve.wait_ge(evac, i * 2 + (2 * pair0 + 3))
                dve.tensor_tensor(work[0][:, 0:3 * A_N], work[0][:, 0:3 * A_N], raw[0][:, 0:3 * A_N],
                                  ALU.mult).then_inc(gate_mul, 1)
                split_low(i * 2 + (2 * pair0 + 2), 0)
                dve.wait_ge(evac, i * 2 + (2 * pair0 + 4))
                dve.wait_ge(gate_mul, i + (pair0 - ZA[0] + 1))
                dve.wait_ge(stored[0], i * 16 + (16 * pair0 + 16))
                out = stage[0][:, A_COL:T]
                if norm:
                    dve.scalar_tensor_tensor(out=out, in0=work[0][:, 0:3 * A_N], scalar=par[:, PAR_GN:PAR_GN + 1],
                                             in1=work[1][:, 0:3 * A_N], op0=ALU.mult,
                                             op1=ALU.mult).then_inc(gated, 1)
                else:
                    dve.tensor_tensor(out, work[0][:, 0:3 * A_N], work[1][:, 0:3 * A_N],
                                      ALU.mult).then_inc(gated, 1)
                split_low(i * 2 + (2 * pair0 + 3), 1)

            with dve.Fori(0, ZA[1]) as i:
                gate(i, ZA[0], S_ZA, True)
            with dve.Fori(0, ZB[1]) as i:
                gate(i, ZB[0], S_ZB, False)
            cos, sin = rope[:, 0, :], rope[:, 1, :]
            dve.wait_ge(rope_in, 16)
            with dve.Fori(0, ROT[1]) as i:
                x1, x2 = raw[0][:, 4:4 + N], raw[1][:, 4:4 + N]
                a, b = work[0][:, 0:N], work[1][:, 0:N]
                dve.wait_ge(evac, i * 2 + (2 * ROT[0] + 4))
                dve.tensor_tensor(a, x1, cos, ALU.mult).then_inc(rot_mul, 1)
                dve.tensor_tensor(b, x2, sin, ALU.mult).then_inc(rot_mul, 1)
                split_low(i * 2 + (2 * ROT[0] + 2), 0)
                dve.wait_ge(rot_mul, i * 5 + 2)
                dve.wait_ge(stored[0], i * 16 + 16 * (ROT[0] + 1))
                dve.tensor_tensor(stage[0][:, PAD:T], a, b, ALU.subtract).then_inc(rot_mul, 1)
                split_low(i * 2 + (2 * ROT[0] + 3), 1)
                dve.wait_ge(rot_mul, i * 5 + 3)
                dve.tensor_tensor(a, x2, cos, ALU.mult).then_inc(rot_mul, 1)
                dve.tensor_tensor(b, x1, sin, ALU.mult).then_inc(rot_mul, 1)
                dve.wait_ge(rot_mul, i * 5 + 5)
                dve.wait_ge(stored[1], i * 16 + 16 * (ROT[0] - 15))
                dve.tensor_tensor(stage[1][:, PAD:T], a, b, ALU.add).then_inc(rotated, 1)
            with dve.Fori(0, RV[1] - 1) as i:
                for s in range(SLOTS):
                    split_low(i * 2 + (2 * RV[0] + s + 2), s)
            split_low(NT, 0)
            turned_gates = psum[:, 6, 0:NCH * 2 * GH].rearrange("p (c g) -> p c g", c=NCH)
            dve.wait_ge(ab_turned, 1)
            dve.tensor_tensor(gtmp[:, :, 0:GH], turned_gates[:, :, 0:GH],
                              arow[:, 1:2, :].broadcast_to((P, NCH, GH)), ALU.add).then_inc(ab_step, 1)
            dve.wait_ge(ab_step, 6)
            dve.tensor_scalar(gtmp[:, :, GH:2 * GH], gtmp[:, :, GH:2 * GH], 1.0, None, ALU.add).then_inc(ab_step, 1)
            dve.scalar_tensor_tensor(out=gabs[:, :, :], in0=gtmp[:, :, 0:GH], scalar=0.0, in1=gabs[:, :, :],
                                     op0=ALU.max, op1=ALU.add).then_inc(ab_step, 1)
            dve.wait_ge(ab_step, 8)
            dve.reciprocal(gates[:, :, GH:2 * GH], gtmp[:, :, GH:2 * GH]).then_inc(ab_step, 1)
            dve.tensor_tensor(gtmp[:, :, 0:GH], gabs[:, :, :],
                              rate[:, :].rearrange("p (a g) -> p a g", a=1).broadcast_to((P, NCH, GH)),
                              ALU.mult).then_inc(ab_step, 1)
            dve.wait_ge(ab_step, 10)
            dve.tensor_scalar(gates[:, :, 0:GH], gtmp[:, :, 0:GH], -1.0, None, ALU.mult).then_inc(ab_step, 1)
            dve.wait_ge(ab_step, 11)
            dve.memset(gates[0:PAD, 0, 0:GH], 0.0).then_inc(ab_step, 1)

        @block.gpsimd
        def _(pool):
            pool.memset(abT[:, 0:A_COL], 0.0).then_inc(ab_raw, 1)
            for c in range(NCH):
                h = hT[:, :, c * CH:c * CH + CH]
                pool.wait_ge(hT_out, c + 1)
                if c >= 2:
                    pool.wait_ge(summed, c - 1)
                pool.tensor_tensor(sq[:, c % 2, :, :], h, h, ALU.mult).then_inc(squared, 1)


class Stage:

    def __init__(self, sem, per, unit=1):
        self.sem, self.per, self.unit = sem, per, unit

    def open(self, eng):
        eng.sem_inc(self.sem, self.per * self.unit)

    def now(self, eng, c, steps=None):
        steps = self.per if steps is None else steps
        eng.wait_ge(self.sem, c * (self.per * self.unit) + (self.per + steps) * self.unit)

    def before(self, eng, c, steps=None):
        steps = self.per if steps is None else steps
        eng.wait_ge(self.sem, c * (self.per * self.unit) + steps * self.unit)


def mixer_phase(nc, io, sc, y):
    with ExitStack() as ctx:
        def sb(name, shape, dt=F32):
            return ctx.enter_context(nc.sbuf_tensor(name, shape, dt))

        psum = ctx.enter_context(nc.psum_tensor("b_psum", [P, 8, 512], F32))
        cst = sb("b_cst", [P, C_W_ALL])
        gates = sb("b_gates", [P, NCH, 2 * GH])
        gc = sb("gates_chunk", [P, 2 * GH])
        qk_in = sb("qk_in", [P, 16, CH])
        v_in = sb("v_in", [P, 8, CH])
        z_in = sb("z_in", [P, 16, CH])
        r_in = sb("r_in", [P, 24, CH])
        qk = sb("qk_normed", [P, 16, CH])
        sq = sb("qk_squares", [P, 16, CH])
        rr = sb("qk_norms", [P, 16, CH])
        ug = sb("log_g_spread", [P, GH, CH])
        gcol = sb("g_col", [P, GH])
        egcol = sb("exp_g_col", [P, GH])
        beg = sb("beta_exp_g", [P, GH])
        dT = sb("decay_T", [P, GH, CH])
        dN = sb("decay_N", [P, GH, CH])
        eg = sb("exp_g_row", [P, GH, CH])
        M = sb("M", [P, GH, CH])
        attn = sb("attn_T", [P, GH, CH])
        XT = sb("XT", [P, GH, CH])
        X = sb("X", [P, GH, CH])
        Q = sb("Q", [P, GH, 64])
        vb = sb("v_beta", [P, GH, CH])
        kbg = sb("k_beta_exp_g", [P, GH, CH])
        kd = sb("k_decayed", [P, GH, CH])
        wT = sb("minus_w_T", [P, GH, CH])
        vnew = sb("v_new", [P, GH, CH])
        qd = sb("q_decayed", [P, GH, CH])
        S = sb("S", [P, GH, P])
        osq = sb("o_squares", [P, GH, CH])
        ro = sb("o_norms", [P, GH, CH])
        oz = sb("o_gated", [P, GH, CH])
        rsc = sb("r_scores", [P, RH, CH])
        rkd = sb("r_k_decayed", [P, RH, 256])
        rv = sb("r_v", [P, RH, 256])
        rqd = sb("r_q_decayed", [P, 8, CH])
        rS = sb("r_S", [P, RH, 2, 256])
        rosq = sb("r_o_squares", [P, 8, CH])
        rro = sb("r_o_norms", [P, RH, CH])
        roz = sb("r_o_gated", [P, 8, CH])

        stages = []

        def stage(name, per, unit=1):
            st = Stage(ctx.enter_context(nc.semaphore(name)), per, unit)
            stages.append(st)
            return st

        tables = ctx.enter_context(nc.semaphore("b_tables"))
        s_zero = ctx.enter_context(nc.semaphore("s_zero"))
        qk_load, v_load = stage("qk_load", 1, 16), stage("v_load", 1, 16)
        z_load, r_load = stage("z_load", 1, 16), stage("r_load", 1, 16)
        g_spread, x_init, q_dec, r_qdec = (stage(n, k) for n, k in (
            ("g_spread", 2), ("x_init", 1), ("q_dec", 1), ("r_qdec", 1)))
        (pe_ss, pe_g, pe_rsc, pe_qk, pe_tr, pe_Q, pe_R, pe_T, pe_rtr, pe_ro, pe_rss, pe_rS, pe_w, pe_u, pe_o, pe_S,
         pe_oss) = (stage(n, k) for n, k in (
            ("pe_ss", 2), ("pe_g", 2), ("pe_rsc", 1), ("pe_qk", 4), ("pe_tr", 2), ("pe_Q", 14), ("pe_R", 12),
            ("pe_T", 12), ("pe_rtr", 2), ("pe_ro", 1), ("pe_rss", 1), ("pe_rS", 1), ("pe_w", 2), ("pe_u", 2),
            ("pe_o", 2), ("pe_S", 2), ("pe_oss", 2)))
        (a_sq, a_ln, a_norm, a_egcol, a_decay, a_eg, a_X, a_w, a_v, a_osq, a_oln, a_onorm, a_rv, a_rosq, a_roln,
         a_ronorm) = (stage(n, k) for n, k in (
            ("a_sq", 2), ("a_ln", 2), ("a_norm", 2), ("a_egcol", 1), ("a_decay", 2), ("a_eg", 1), ("a_X", 12),
            ("a_w", 2), ("a_v", 2), ("a_osq", 2), ("a_oln", 1), ("a_onorm", 1), ("a_rv", 1), ("a_rosq", 1),
            ("a_roln", 1), ("a_ronorm", 1)))
        (d_gcol, d_diff, d_qk, d_beg, d_attn, d_M, d_Q, d_XT, d_vb, d_kbg, d_kd, d_S, d_oz, d_y, d_rsc, d_rkd,
         d_rS, d_roz, d_ry, d_sum) = (stage(n, k) for n, k in (
            ("d_gcol", 1), ("d_diff", 16), ("d_qk", 2), ("d_beg", 1), ("d_attn", 4), ("d_M", 8), ("d_Q", 14),
            ("d_XT", 14), ("d_vb", 2), ("d_kbg", 2), ("d_kd", 2), ("d_S", 8), ("d_oz", 2), ("d_y", 1),
            ("d_rsc", 1), ("d_rkd", 1), ("d_rS", 4), ("d_roz", 1), ("d_ry", 1), ("d_sum", 1)))
        block = ctx.enter_context(nc.Block())

        def const(at, n):
            return cst[:, at:at + n]

        ident, ones = const(C_ID, P), const(C_ONES, P)
        eps, lnq = const(C_EPS, 1), const(C_LNQ, 1)

        def odd(x, g, lv):
            return x[:, 4 * g:4 * g + 4, :].rearrange("p h (n t b) -> p (h n) t b", t=2, b=1 << lv)[:, :, 1, :]

        def heads(g):
            return slice(4 * g, 4 * g + 4)

        def four(bank):
            return psum[:, bank, :].rearrange("p (h c) -> p h c", h=4)

        @block.sync
        def _(sp):
            sp.dma_start(cst[:, :], io["cst"]).then_inc(tables, 16)
            sp.dma_start(gates[:, :, :], sc["gates"]).then_inc(tables, 16)
            for st in (qk_load, v_load, z_load, r_load):
                st.open(sp)
            mix = sc["mix"].rearrange("s p c -> p s c")
            with sp.Fori(0, NCH) as c:
                col = sp.snap(c * CH)

                def load(st, buf, first, n):
                    sp.dma_start(buf[:, :, :], mix[:, first:first + n, bass.ds(col, CH)]).then_inc(st.sem, 16)

                a_sq.before(sp, c)
                d_qk.before(sp, c)
                load(qk_load, qk_in, S_Q, 16)
                r_qdec.before(sp, c)
                pe_rsc.before(sp, c)
                pe_rtr.before(sp, c)
                load(r_load, r_in, S_RQ, 24)
                pe_tr.before(sp, c)
                load(v_load, v_in, S_V, 8)
                d_roz.before(sp, c)
                d_oz.before(sp, c)
                load(z_load, z_in, S_ZA, 16)

        @block.gpsimd
        def _(pool):
            for st in (g_spread, x_init, q_dec, r_qdec):
                st.open(pool)
            pool.memset(S[:, :, :], 0.0).then_inc(s_zero, 1)
            pool.memset(rS[:, :, :, :], 0.0).then_inc(s_zero, 1)
            pool.wait_ge(tables, 32)
            with pool.Fori(0, NCH) as c:
                pe_g.before(pool, c)
                d_M.before(pool, c)
                d_vb.before(pool, c)
                pool.tensor_tensor(gc[:, :].rearrange("p (o g) -> p o g", o=1), gates[:, bass.ds(c, 1), :],
                                   const(C_ONES, 2 * GH).rearrange("p (o g) -> p o g", o=1),
                                   ALU.mult).then_inc(g_spread.sem, 1)
                g_spread.now(pool, c, 1)
                pool.tensor_tensor(ug[:, :, :],
                                   const(C_TRIU, P).rearrange("p (o c) -> p o c", o=1).broadcast_to((P, GH, CH)),
                                   gc[:, 0:GH].rearrange("p (g o) -> p g o", o=1).broadcast_to((P, GH, CH)),
                                   ALU.mult).then_inc(g_spread.sem, 1)
                pe_u.before(pool, c)
                pool.tensor_tensor(XT[:, :, :], ident.rearrange("p (o c) -> p o c", o=1).broadcast_to((P, GH, CH)),
                                   ones.rearrange("p (o c) -> p o c", o=1).broadcast_to((P, GH, CH)),
                                   ALU.mult).then_inc(x_init.sem, 1)
                r_load.now(pool, c)
                pe_ro.before(pool, c)
                rq = r_in[:, 0:8, :].rearrange("p (h a) c -> p h a c", a=2)
                row = const(C_RROW, RH * CH).rearrange("p (h o c) -> p h o c", h=RH, o=1)
                pool.tensor_tensor(rqd[:, :, :].rearrange("p (h a) c -> p h a c", a=2), rq,
                                   row.broadcast_to((P, RH, 2, CH)), ALU.mult).then_inc(r_qdec.sem, 1)
                a_eg.now(pool, c)
                d_qk.now(pool, c)
                pe_o.before(pool, c)
                pool.tensor_tensor(qd[:, :, :], qk[:, 0:8, :], eg[:, :, :], ALU.mult).then_inc(q_dec.sem, 1)

        @block.tensor
        def _(pe):
            for st in (pe_ss, pe_g, pe_rsc, pe_qk, pe_tr, pe_Q, pe_R, pe_T, pe_rtr, pe_ro, pe_rss, pe_rS, pe_w, pe_u,
                       pe_o, pe_S, pe_oss):
                st.open(pe)
            pe.wait_ge(tables, 32)
            pe.wait_ge(s_zero, 2)
            with pe.Fori(0, NCH) as c:
                a_oln.before(pe, c)
                a_v.before(pe, c)
                for half in range(2):
                    a_sq.now(pe, c, half + 1)
                    for b in range(2):
                        n = 2 * half + b
                        mm = pe.matmul(psum[:, n, :], ones, sq[:, 4 * n:4 * n + 4, :], start=True, stop=True)
                    mm.then_inc(pe_ss.sem, 1)
                g_spread.now(pe, c)
                d_oz.before(pe, c)
                d_S.before(pe, c)
                pe.matmul(psum[:, 6, 0:GH], const(C_TRIU, P), gc[:, 0:GH], start=True, stop=True).then_inc(pe_g.sem, 1)
                for g in range(2):
                    mm = pe.matmul(psum[:, 4 + g, :], ones, ug[:, heads(g), :], start=True, stop=True)
                mm.then_inc(pe_g.sem, 1)
                r_load.now(pe, c)
                for h in range(RH):
                    for a in range(2):
                        mm = pe.matmul(psum[:, 7, h * CH:(h + 1) * CH], r_in[:, 8 + 2 * h + a, :],
                                       r_in[:, 2 * h + a, :], start=(a == 0), stop=(a == 1))
                mm.then_inc(pe_rsc.sem, 1)
                d_qk.now(pe, c)
                a_ln.now(pe, c)
                pairs = qk[:, :, :].rearrange("p (w h) c -> p w h c", w=2)
                for h in range(GH):
                    mm = pe.matmul(psum[:, h // 2, (h % 2) * 256:(h % 2) * 256 + 256].rearrange(
                        "p (w c) -> p w c", w=2), qk[:, 8 + h, :], pairs[:, :, h, :], start=True, stop=True)
                    if h % 2:
                        mm.then_inc(pe_qk.sem, 1)

                def turn_qkv():
                    v_load.now(pe, c)
                    d_attn.now(pe, c)
                    d_M.now(pe, c)
                    for src, first, bank in ((v_in, 0, 0), (qk, 8, 2)):
                        for h in range(GH):
                            mm = pe.transpose(psum[:, bank + h // 4, (h % 4) * P:(h % 4) * P + P],
                                              src[:, first + h, :], ident)
                        mm.then_inc(pe_tr.sem, 1)

                def turn_retention():
                    d_vb.now(pe, c)
                    d_kbg.now(pe, c)
                    d_kd.now(pe, c)
                    for first, bank in ((8, 0), (16, 2)):
                        for t in range(8):
                            mm = pe.transpose(psum[:, bank + t // 4, (t % 4) * P:(t % 4) * P + P],
                                              r_in[:, first + t, :], ident)
                        mm.then_inc(pe_rtr.sem, 1)

                def retention_out():
                    d_rkd.now(pe, c)
                    a_rv.now(pe, c)
                    d_rsc.now(pe, c)
                    r_qdec.now(pe, c)
                    d_rS.before(pe, c)
                    for h in range(RH):
                        for e in range(2):
                            t = 2 * h + e
                            o = psum[:, t // 4, (t % 4) * CH:(t % 4) * CH + CH]
                            pe.matmul(o, rv[:, h, e * P:e * P + P], rsc[:, h, :], start=True, stop=False)
                            for a in range(2):
                                mm = pe.matmul(o, rS[:, h, a, e * P:e * P + P], rqd[:, 2 * h + a, :],
                                               start=False, stop=(a == 1))
                    mm.then_inc(pe_ro.sem, 1)

                def retention_norm():
                    a_rosq.now(pe, c)
                    for h in range(RH):
                        for e in range(2):
                            mm = pe.matmul(psum[:, 2, h * CH:(h + 1) * CH], ones, rosq[:, 2 * h + e, :],
                                           start=(e == 0), stop=(e == 1))
                    mm.then_inc(pe_rss.sem, 1)

                def retention_state():
                    d_roz.now(pe, c)
                    a_roln.now(pe, c)
                    for h in range(RH):
                        for a in range(2):
                            mm = pe.matmul(psum[:, h, a * 256:a * 256 + 256], rkd[:, h, a * P:a * P + P],
                                           rv[:, h, :], start=True, stop=True)
                    mm.then_inc(pe_rS.sem, 1)

                x_init.now(pe, c)
                a_eg.now(pe, c)
                d_gcol.now(pe, c)
                d_rsc.now(pe, c)
                fill = {0: turn_qkv, 1: turn_retention, 2: retention_out, 3: retention_norm, 4: retention_state}
                for lv in range(NLEVEL):
                    for g in range(2):
                        if lv:
                            d_XT.now(pe, c, 2 * lv - 1 + g)
                            for h in range(4):
                                mm = pe.transpose(psum[:, 6 + g, h * P:h * P + P], XT[:, 4 * g + h, :], ident)
                            mm.then_inc(pe_T.sem, 1)
                        d_M.now(pe, c, 4 * g + 4)
                        for h in range(4):
                            rhs = XT[:, 4 * g + h, :].rearrange("p (n t b) -> p n t b", t=2, b=1 << lv)[:, :, 1, :]
                            out = psum[:, 4 + g, h * 64:h * 64 + 64].rearrange("p (n b) -> p n b", b=1 << lv)
                            mm = pe.matmul(out, M[:, 4 * g + h, :], rhs, start=True, stop=True)
                        mm.then_inc(pe_Q.sem, 1)
                    if lv in fill:
                        fill[lv]()
                    if lv:
                        for g in range(2):
                            a_X.now(pe, c, 2 * lv - 1 + g)
                            d_Q.now(pe, c, 2 * lv + 1 + g)
                            for h in range(4):
                                mm = pe.matmul(psum[:, 4 + g, 256 + h * 64:256 + h * 64 + 64], X[:, 4 * g + h, :],
                                               Q[:, 4 * g + h, :], start=True, stop=True)
                            mm.then_inc(pe_R.sem, 1)
                d_rS.now(pe, c)
                d_kbg.now(pe, c)
                for g in range(2):
                    d_XT.now(pe, c, 13 + g)
                    for h in range(4):
                        mm = pe.matmul(psum[:, g, h * CH:(h + 1) * CH], kbg[:, 4 * g + h, :], XT[:, 4 * g + h, :],
                                       start=True, stop=True)
                    mm.then_inc(pe_w.sem, 1)
                d_vb.now(pe, c)
                d_S.before(pe, c)
                for g in range(2):
                    a_w.now(pe, c, g + 1)
                    for h in range(4 * g, 4 * g + 4):
                        o = psum[:, 2 + g, (h % 4) * P:(h % 4) * P + P]
                        pe.matmul(o, XT[:, h, :], vb[:, h, :], start=True, stop=False)
                        mm = pe.matmul(o, wT[:, h, :], S[:, h, :], start=False, stop=True)
                    mm.then_inc(pe_u.sem, 1)
                q_dec.now(pe, c)
                for g in range(2):
                    a_v.now(pe, c, g + 1)
                    for h in range(4 * g, 4 * g + 4):
                        o = psum[:, 4 + g, (h % 4) * CH:(h % 4) * CH + CH]
                        pe.matmul(o, S[:, h, :], qd[:, h, :], start=True, stop=False)
                        mm = pe.matmul(o, vnew[:, h, :], attn[:, h, :], start=False, stop=True)
                    mm.then_inc(pe_o.sem, 1)
                    for h in range(4 * g, 4 * g + 4):
                        mm = pe.matmul(psum[:, 6 + g, (h % 4) * P:(h % 4) * P + P], kd[:, h, :], vnew[:, h, :],
                                       start=True, stop=True)
                    mm.then_inc(pe_S.sem, 1)
                for g in range(2):
                    a_osq.now(pe, c, g + 1)
                    pe.matmul(psum[:, g, :], ones, osq[:, heads(g), :], start=True, stop=True).then_inc(pe_oss.sem, 1)

        @block.scalar
        def _(act):
            for st in (a_sq, a_ln, a_norm, a_egcol, a_decay, a_eg, a_X, a_w, a_v, a_osq, a_oln, a_onorm, a_rv, a_rosq,
                       a_roln, a_ronorm):
                st.open(act)
            act.preload_act_table_set("natural_log_exp_and_others")
            act.wait_ge(tables, 32)
            with act.Fori(0, NCH) as c:
                qk_load.now(act, c)
                pe_ss.before(act, c)
                for half in range(2):
                    w = slice(8 * half, 8 * half + 8)
                    act.activation(sq[:, w, :], qk_in[:, w, :], ACT.Square).then_inc(a_sq.sem, 1)
                d_gcol.now(act, c)
                d_beg.before(act, c)
                act.activation(egcol[:, :], gcol[:, :], ACT.Exp).then_inc(a_egcol.sem, 1)
                d_qk.before(act, c)
                for half in range(2):
                    w = slice(8 * half, 8 * half + 8)
                    pe_ss.now(act, c, half + 1)
                    act.activation(rr[:, w, :].rearrange("p (b h) c -> p b (h c)", b=2),
                                   psum[:, 2 * half:2 * half + 2, :], ACT.Ln, bias=eps).then_inc(a_ln.sem, 1)
                    a_ln.now(act, c, half + 1)
                    act.activation(rr[:, w, :], rr[:, w, :], ACT.Exp, scale=-0.5,
                                   bias=0.0 if half else lnq).then_inc(a_norm.sem, 1)
                d_diff.now(act, c)
                act.activation(dT[:, :, :], dT[:, :, :], ACT.Exp).then_inc(a_decay.sem, 1)
                act.activation(dN[:, :, :], dN[:, :, :], ACT.Exp, scale=-1.0).then_inc(a_decay.sem, 1)
                d_S.before(act, c)
                q_dec.before(act, c)
                act.activation(eg[:, :, :].rearrange("p (b h) c -> p b (h c)", b=2), psum[:, 4:6, :],
                               ACT.Exp).then_inc(a_eg.sem, 1)

                def retention_v():
                    pe_rtr.now(act, c, 2)
                    pe_rS.before(act, c)
                    pe_ro.before(act, c)
                    act.activation(rv[:, :, :].rearrange("p (b h) c -> p b (h c)", b=2), psum[:, 2:4, :],
                                   ACT.Copy).then_inc(a_rv.sem, 1)

                def retention_squares():
                    pe_ro.now(act, c)
                    pe_rss.before(act, c)
                    act.activation(rosq[:, :, :].rearrange("p (b h) c -> p b (h c)", b=2), psum[:, 0:2, :],
                                   ACT.Square).then_inc(a_rosq.sem, 1)

                def retention_norms():
                    pe_rss.now(act, c)
                    d_ry.before(act, c)
                    act.activation(rro[:, :, :], four(2), ACT.Ln, bias=eps, scale=1.0 / 256).then_inc(a_roln.sem, 1)
                    a_roln.now(act, c)
                    act.activation(rro[:, :, :], rro[:, :, :], ACT.Exp, scale=-0.5).then_inc(a_ronorm.sem, 1)

                fill = {2: retention_v, 3: retention_squares, 4: retention_norms}
                for lv in range(1, NLEVEL):
                    for g in range(2):
                        pe_T.now(act, c, 2 * lv - 1 + g)
                        if lv > 1:
                            pe_R.now(act, c, 2 * lv - 3 + g)
                        else:
                            pe_R.before(act, c)
                        act.activation(X[:, heads(g), :], four(6 + g), ACT.Copy).then_inc(a_X.sem, 1)
                    if lv in fill:
                        fill[lv]()
                for g in range(2):
                    pe_w.now(act, c, g + 1)
                    pe_u.before(act, c)
                    act.activation(wT[:, heads(g), :], four(g), ACT.Copy, scale=-1.0).then_inc(a_w.sem, 1)
                for g in range(2):
                    pe_u.now(act, c, g + 1)
                    pe_o.before(act, c)
                    pe_S.before(act, c)
                    act.activation(vnew[:, heads(g), :], four(2 + g), ACT.Copy).then_inc(a_v.sem, 1)
                for g in range(2):
                    pe_o.now(act, c, g + 1)
                    pe_oss.before(act, c)
                    act.activation(osq[:, heads(g), :], four(4 + g), ACT.Square).then_inc(a_osq.sem, 1)
                pe_oss.now(act, c)
                d_y.before(act, c)
                act.activation(ro[:, :, :].rearrange("p (b h) c -> p b (h c)", b=2), psum[:, 0:2, :], ACT.Ln,
                               bias=eps, scale=1.0 / P).then_inc(a_oln.sem, 1)
                a_oln.now(act, c)
                act.activation(ro[:, :, :], ro[:, :, :], ACT.Exp, scale=-0.5).then_inc(a_onorm.sem, 1)

        @block.vector
        def _(dve):
            for st in (d_gcol, d_diff, d_qk, d_beg, d_attn, d_M, d_Q, d_XT, d_vb, d_kbg, d_kd, d_S, d_oz, d_y, d_rsc,
                       d_rkd, d_rS, d_roz, d_ry, d_sum):
                st.open(dve)
            dve.wait_ge(tables, 32)
            dve.wait_ge(s_zero, 2)
            with dve.Fori(0, NCH) as c:
                pe_g.now(dve, c, 1)
                d_diff.before(dve, c)
                a_egcol.before(dve, c)
                dve.tensor_copy(gcol[:, :], psum[:, 6, 0:GH]).then_inc(d_gcol.sem, 1)
                pe_g.now(dve, c, 2)
                d_gcol.now(dve, c)
                d_attn.before(dve, c)
                d_M.before(dve, c)
                d_kd.before(dve, c)
                for out, bound, op in ((dT, C_UPTO, ALU.min), (dN, C_BELOW, ALU.max)):
                    for h in range(GH):
                        dve.scalar_tensor_tensor(out=out[:, h, :], in0=four(4 + h // 4)[:, h % 4, :],
                                                 scalar=gcol[:, h:h + 1], in1=const(bound, P), op0=ALU.subtract,
                                                 op1=op).then_inc(d_diff.sem, 1)
                a_egcol.now(dve, c)
                d_kbg.before(dve, c)
                dve.tensor_tensor(beg[:, :], egcol[:, :], gc[:, GH:2 * GH], ALU.mult).then_inc(d_beg.sem, 1)
                pe_rsc.now(dve, c)
                pe_ro.before(dve, c)
                dve.tensor_tensor(rsc[:, :, :], four(7), const(C_RDEC, RH * CH).rearrange(
                    "p (h c) -> p h c", h=RH), ALU.mult).then_inc(d_rsc.sem, 1)
                pe_tr.before(dve, c)
                q_dec.before(dve, c)
                for half in range(2):
                    w = slice(8 * half, 8 * half + 8)
                    a_norm.now(dve, c, half + 1)
                    dve.tensor_tensor(qk[:, w, :], qk_in[:, w, :], rr[:, w, :], ALU.mult).then_inc(d_qk.sem, 1)
                a_decay.now(dve, c)
                pe_o.before(dve, c)
                pe_Q.before(dve, c)
                for b in range(4):
                    pe_qk.now(dve, c, b + 1)
                    qk2 = four(b)
                    for h in range(2 * b, 2 * b + 2):
                        dve.scalar_tensor_tensor(out=M[:, h, :], in0=qk2[:, 2 * (h % 2) + 1, :],
                                                 scalar=gc[:, GH + h:GH + h + 1], in1=dN[:, h, :], op0=ALU.mult,
                                                 op1=ALU.mult).then_inc(d_M.sem, 1)
                for b in range(4):
                    dve.tensor_tensor(attn[:, 2 * b:2 * b + 2, :],
                                      four(b).rearrange("p (h w) c -> p h w c", w=2)[:, :, 0, :],
                                      dT[:, 2 * b:2 * b + 2, :], ALU.mult).then_inc(d_attn.sem, 1)

                def spread(col):
                    return col.rearrange("p (h o) -> p h o", o=1).broadcast_to((P, 4, CH))

                def delta_kv():
                    pe_u.before(dve, c)
                    pe_w.before(dve, c)
                    pe_S.before(dve, c)
                    d_beg.now(dve, c)
                    for g in range(2):
                        pe_tr.now(dve, c, 1)
                        dve.tensor_tensor(vb[:, heads(g), :], four(g), spread(gc[:, GH + 4 * g:GH + 4 * g + 4]),
                                          ALU.mult).then_inc(d_vb.sem, 1)
                    for g in range(2):
                        pe_tr.now(dve, c, 2)
                        dve.tensor_tensor(kbg[:, heads(g), :], four(2 + g), spread(beg[:, 4 * g:4 * g + 4]),
                                          ALU.mult).then_inc(d_kbg.sem, 1)
                        dve.tensor_tensor(kd[:, heads(g), :], four(2 + g),
                                          dT[:, heads(g), CH - 1:CH].broadcast_to((P, 4, CH)),
                                          ALU.mult).then_inc(d_kd.sem, 1)

                def retention_k():
                    pe_rtr.now(dve, c, 1)
                    pe_rS.before(dve, c)
                    col = const(C_RCOL, RH).rearrange("p (h o) -> p h o", o=1).broadcast_to((P, RH, 256))
                    dve.tensor_tensor(rkd[:, :, :], psum[:, 0:2, :].rearrange("p b (h c) -> p (b h) c", h=2), col,
                                      ALU.mult).then_inc(d_rkd.sem, 1)

                def retention_gate():
                    z_load.now(dve, c)
                    a_rosq.now(dve, c)
                    d_ry.before(dve, c)
                    dve.tensor_tensor(roz[:, :, :], psum[:, 0:2, :].rearrange("p b (h c) -> p (b h) c", h=4),
                                      z_in[:, 8:16, :], ALU.mult).then_inc(d_roz.sem, 1)

                def retention_y():
                    a_ronorm.now(dve, c)
                    d_roz.now(dve, c)
                    dve.tensor_tensor(roz[:, :, :].rearrange("p (h e) c -> p h e c", e=2),
                                      roz[:, :, :].rearrange("p (h e) c -> p h e c", e=2),
                                      rro[:, :, :].rearrange("p h (o c) -> p h o c", o=1).broadcast_to(
                                          (P, RH, 2, CH)), ALU.mult).then_inc(d_ry.sem, 1)

                def retention_state():
                    pe_rS.now(dve, c)
                    for h in range(RH):
                        keep = math.exp(CH * math.log(1.0 - 2.0 ** (-5.0 - h)))
                        s_all = rS[:, h, :, :].rearrange("p a e -> p (a e)")
                        dve.scalar_tensor_tensor(out=s_all, in0=s_all, scalar=keep, in1=psum[:, h, :], op0=ALU.mult,
                                                 op1=ALU.add).then_inc(d_rS.sem, 1)

                fill = {0: delta_kv, 1: retention_k, 3: retention_gate, 4: retention_y, 5: retention_state}
                x_init.now(dve, c)
                for lv in range(NLEVEL):
                    for g in range(2):
                        pe_Q.now(dve, c, 2 * lv + 1 + g)
                        if lv > 1:
                            pe_R.now(dve, c, 2 * lv - 3 + g)
                        elif lv == 0:
                            pe_R.before(dve, c)
                            d_XT.before(dve, c)
                        else:
                            d_XT.now(dve, c, g + 1)
                        mask = const(C_LEVEL + 64 * lv, 64).rearrange("p (o c) -> p o c", o=1)
                        dve.tensor_tensor(Q[:, heads(g), :], psum[:, 4 + g, 0:256].rearrange("p (h c) -> p h c", h=4),
                                          mask.broadcast_to((P, 4, 64)), ALU.mult).then_inc(d_Q.sem, 1)
                    if lv in fill:
                        fill[lv]()
                    for g in range(2):
                        b = 1 << lv
                        if lv:
                            pe_R.now(dve, c, 2 * lv - 1 + g)
                            more = psum[:, 4 + g, 256:512].rearrange("p (n b) -> p n b", b=b)
                        else:
                            d_Q.now(dve, c, g + 1)
                            more = Q[:, heads(g), :].rearrange("p h (n b) -> p (h n) b", b=b)
                        dve.tensor_tensor(odd(XT, g, lv), odd(XT, g, lv), more, ALU.add).then_inc(d_XT.sem, 1)
                for g in range(2):
                    pe_S.now(dve, c, g + 1)
                    for h in range(4 * g, 4 * g + 4):
                        dve.scalar_tensor_tensor(out=S[:, h, :], in0=S[:, h, :], scalar=eg[:, h, CH - 1:CH],
                                                 in1=four(6 + g)[:, h % 4, :], op0=ALU.mult,
                                                 op1=ALU.add).then_inc(d_S.sem, 1)
                d_sum.before(dve, c)
                for g in range(2):
                    a_osq.now(dve, c, g + 1)
                    dve.tensor_tensor(oz[:, heads(g), :], four(4 + g), z_in[:, heads(g), :],
                                      ALU.mult).then_inc(d_oz.sem, 1)
                a_onorm.now(dve, c)
                d_oz.now(dve, c)
                dve.tensor_tensor(oz[:, :, :], oz[:, :, :], ro[:, :, :], ALU.mult).then_inc(d_y.sem, 1)
                d_y.now(dve, c)
                d_ry.now(dve, c)
                dve.tensor_tensor(y[:, :, bass.ds(c * CH, CH)], oz[:, :, :], roz[:, :, :],
                                  ALU.add).then_inc(d_sum.sem, 1)


def output_phase(nc, io, sc, y, out):
    with ExitStack() as ctx:
        def sb(name, shape, dt=F32):
            return ctx.enter_context(nc.sbuf_tensor(name, shape, dt))

        def sem(name):
            return ctx.enter_context(nc.semaphore(name))

        psum = ctx.enter_context(nc.psum_tensor("c_psum", [P, 8, 512], F32))
        cst = sb("c_cst", [P, C_EPS + 1])
        par = sb("c_par", [P, PAR_W])
        gf = sb("norm_f_rows", [P, D])
        xh = sb("c_xh", [P, KC, C_W], F32R)
        xl = sb("c_xl", [P, KC, C_W], F32R)
        h = sb("residual_T", [P, KC, C_W])
        wraw = [sb(f"c_w_raw{s}", [P, KC, P]) for s in range(SLOTS)]
        wh = [sb(f"c_w_hi{s}", [P, KC, P], F32R) for s in range(SLOTS)]
        wl = [sb(f"c_w_lo{s}", [P, KC, P], F32R) for s in range(SLOTS)]
        draw = sb("down_raw", [P, D])
        dh = sb("down_hi", [P, D], F32R)
        dl = sb("down_lo", [P, D], F32R)
        ah = [sb(f"act_hi{s}", [P, SEQ], F32R) for s in range(SLOTS)]
        al = [sb(f"act_lo{s}", [P, SEQ], F32R) for s in range(SLOTS)]
        rsum = sb("row_sums", [P, 8])
        rln = sb("row_logs", [P, 8])
        rnorm = sb("row_norms", [P, 8])
        sq = [y[:, 0, 0:C_W], y[:, 1, 0:C_W]]
        ssq, rbc = y[:, 2, 0:C_W], y[:, 3, 0:C_W]
        xn = [y[:, 4, 0:C_W], y[:, 5, 0:C_W]]
        raw = [y[:, 6, 0:C_W], y[:, 7, 0:C_W]]
        acc = [y[:, 0, 0:SEQ], y[:, 1, 0:SEQ]]
        junk = [y[:, 2, 0:D], y[:, 3, 0:D]]
        rows = [y[:, 4, 0:D], y[:, 5, 0:D]]

        tables, h_in = sem("c_tables"), sem("h_in")
        w_loaded = [sem(f"c_w_loaded{s}") for s in range(SLOTS)]
        (w_hi, w_lo, mm_done, y_hi, y_split, h_added, squared, summed, ss_ready, ln_done, rms_ready, normed, x_hi,
         x_split, evac) = (sem("c_" + n) for n in (
            "w_hi", "w_lo", "mm_done", "y_hi", "y_split", "h_added", "squared", "summed", "ss_ready", "ln_done",
            "rms_ready", "normed", "x_hi", "x_split", "evac"))
        d_loaded, d_hi, d_lo = sem("down_loaded"), sem("down_hi_done"), sem("down_lo_done")
        conv, silu, prod, act_hi, act_lo = (sem("f_" + n) for n in ("conv", "silu", "prod", "act_hi", "act_lo"))
        down, added = sem("f_down"), sem("f_added")
        turned, row_sum, row_ln, row_norm, row_out = (sem("o_" + n) for n in ("turned", "sum", "ln", "norm", "out"))
        row_stored = [sem(f"o_stored{s}") for s in range(SLOTS)]
        block = ctx.enter_context(nc.Block())

        w_out = io["w_out"][0].rearrange("(k p) n -> p k n", p=P)
        w_up = io["w_ffn_up"][0].rearrange("(k p) n -> p k n", p=P)
        w_down = io["w_ffn_down"][0]
        ident, ones = cst[:, C_ID:C_ID + P], cst[:, C_ONES:C_ONES + P]
        eps = cst[:, C_EPS:C_EPS + 1]
        HALVES = 2 * KC
        ADD_BANKS = (6, 7, 0, 1, 2)

        def thirds(x):
            return x.rearrange("p (b c) -> p b c", b=3)

        @block.sync
        def _(sp):
            for s in range(SLOTS):
                sp.dma_start(wraw[s][:, :, :], w_out[:, :, P * s:P * s + P]).then_inc(w_loaded[s], 16)
            sp.dma_start(cst[:, :], io["cst"][:, 0:C_EPS + 1]).then_inc(tables, 16)
            sp.dma_start(par[:, :], sc["par"]).then_inc(tables, 16)
            sp.dma_start(h[:, :, :], sc["hT"][:, :, C_COL:T]).then_inc(h_in, 16)
            sp.dma_start(gf[:, :], io["norm_f"].rearrange("(o d) -> o d", o=1).broadcast_to((P, D))).then_inc(tables, 16)
            sp.dma_start(draw[:, :], w_down[0:P, :]).then_inc(d_loaded, 16)
            for m in range(2, KC):
                sp.wait_ge(w_lo, m - 1)
                sp.dma_start(wraw[m % 2][:, :, :], w_out[:, :, P * m:P * m + P]).then_inc(w_loaded[m % 2], 16)
            for s, col in ((0, 0), (1, D_FF)):
                sp.wait_ge(w_lo, KC - 1 + s)
                sp.dma_start(wraw[s][:, :, :], w_up[:, :, col:col + P]).then_inc(w_loaded[s], 16)

            def load(j):
                a_col, b_col, d_row = sp.snap(j * P), sp.snap(j * P + D_FF), sp.snap(j * P)
                for s, col in ((0, a_col), (1, b_col)):
                    sp.wait_ge(w_lo, j * 2 + (KC - 1 + s))
                    sp.dma_start(wraw[s][:, :, :], w_up[:, :, bass.ds(col, P)]).then_inc(w_loaded[s], 16)
                sp.wait_ge(d_lo, j)
                sp.dma_start(draw[:, :], w_down[bass.ds(d_row, P), :]).then_inc(d_loaded, 16)

            with sp.Fori(1, FT) as j:
                load(j)
            for t in range(SEQ // P):
                sp.wait_ge(row_out, t + 1)
                sp.dma_start(out[0, t * P:t * P + P, :], rows[t % 2]).then_inc(row_stored[t % 2], 16)
            for s in range(SLOTS):
                sp.wait_ge(row_stored[s], 16 * (SEQ // P // 2))

        @block.tensor
        def _(pe):
            for m in range(KC):
                pe.wait_ge(w_lo, m + 1)
                if m >= 2:
                    pe.wait_ge(h_added, m - 1)
                project(pe, psum, 3 * (m % 2), wh[m % 2], wl[m % 2], xh, xl, 0, C_N,
                        y_split if m == 0 else None).then_inc(mm_done, 1)
            pe.wait_ge(tables, 48)
            pe.wait_ge(summed, KC)
            for b in range(3):
                mm = pe.matmul(psum[:, 5 + b, 0:C_N], ones, ssq[:, b * C_N:(b + 1) * C_N], start=True, stop=True)
            mm.then_inc(ss_ready, 1)

            def up(j, s, block_ready=None):
                pe.wait_ge(w_lo, j * 2 + (KC + s + 1))
                if block_ready is None:
                    pe.wait_ge(evac, j * 2 + (s - 1))
                    if s == 0:
                        pe.wait_ge(added, (j - 1) * HALVES)
                project(pe, psum, 3 * s, wh[s], wl[s], xh, xl, 0, C_N, block_ready).then_inc(mm_done, 1)

            def down_product(j, s, first=False, last=False):
                pe.wait_ge(act_lo, j + 1)
                pe.wait_ge(d_lo, j + 1)
                if not last:
                    pe.wait_ge(evac, j * 2 + 3)
                for n in range(HALVES):
                    bank = ADD_BANKS[n % 5]
                    if n >= 5:
                        pe.wait_ge(added, j * HALVES + (n - 4))
                    elif not first:
                        pe.wait_ge(added, j * HALVES)
                    m, half = n // 2, slice((n % 2) * 512, (n % 2) * 512 + 512)
                    for part, (w, x) in enumerate(((dh, ah[s]), (dh, al[s]), (dl, ah[s]))):
                        mm = pe.matmul(psum[:, bank, :], w[:, m * P:m * P + P], x[:, half],
                                       start=(part == 0), stop=(part == 2))
                    mm.then_inc(down, 1)

            pe.wait_ge(rms_ready, 1)
            up(0, 0, x_split)
            pe.wait_ge(h_added, KC)
            pe.wait_ge(w_lo, KC + 2)
            project(pe, psum, 3, wh[1], wl[1], xh, xl, 0, C_N).then_inc(mm_done, 1)
            pe.wait_ge(w_lo, KC + 3)
            pe.wait_ge(evac, 1)
            project(pe, psum, 0, wh[0], wl[0], xh, xl, 0, C_N).then_inc(mm_done, 1)
            up(1, 1)
            down_product(0, 0, True)
            with pe.Fori(1, FT // 2) as i:
                for j, s in ((i * 2, 0), (i * 2 + 1, 1)):
                    up(j, 0)
                    up(j, 1)
                    down_product(j - 1, 1 - s)
            down_product(FT - 1, 1, last=True)
            for t in range(SEQ // P):
                pe.wait_ge(added, FT * HALVES)
                if t >= 4:
                    pe.wait_ge(row_out, t - 3)
                for m in range(KC):
                    mm = pe.transpose(psum[:, 2 * (t % 4) + m // 4, (m % 4) * P:(m % 4) * P + P],
                                      h[:, m, 2 + t * P:2 + t * P + P], ident)
                mm.then_inc(turned, 1)

        @block.scalar
        def _(act):
            act.preload_act_table_set("natural_log_exp_and_others")

            def split_high(n, s):
                act.wait_ge(w_loaded[s], n * 16)
                act.activation(wh[s][:, :, :], wraw[s][:, :, :], ACT.Copy).then_inc(w_hi, 1)

            def y_high(k):
                act.activation(xh[:, k, :], y[:, k, C_COL:T], ACT.Copy).then_inc(y_hi, 1)

            split_high(1, 0)
            y_high(0)
            split_high(1, 1)
            for k in range(1, KC):
                y_high(k)
            for m in range(KC):
                act.wait_ge(mm_done, m + 1)
                split_high(m // 2 + 2, m % 2)
                act.wait_ge(h_added, m + 1)
                act.wait_ge(y_split, KC)
                if m >= 2:
                    act.wait_ge(summed, m - 1)
                o = ssq if m == 0 else sq[m % 2]
                act.activation(o, h[:, m, :], ACT.Square).then_inc(squared, 1)
            act.wait_ge(tables, 48)
            act.wait_ge(ss_ready, 1)
            act.activation(thirds(rbc), psum[:, 5:8, 0:C_N], ACT.Ln, bias=eps, scale=1.0 / D).then_inc(ln_done, 1)
            act.wait_ge(ln_done, 1)
            act.activation(rbc, rbc, ACT.Exp, scale=-0.5).then_inc(rms_ready, 1)
            for k in range(KC):
                act.wait_ge(normed, k + 1)
                act.activation(xh[:, k, :], xn[k % 2], ACT.Copy).then_inc(x_hi, 1)
            act.preload_act_table_set("silu_and_others")

            def down_high(j, first):
                if not first:
                    act.wait_ge(down, j * HALVES)
                act.wait_ge(d_loaded, j * 16 + 16)
                act.activation(dh[:, :], draw[:, :], ACT.Copy).then_inc(d_hi, 1)

            def hidden(j, s, first=False, last=False):
                for half in range(2):
                    act.wait_ge(mm_done, j * 2 + (KC + 1 + half))
                    if not first:
                        act.wait_ge(conv, j * 6 - 3 + 3 * half)
                    act.activation(thirds(raw[half]), psum[:, 3 * half:3 * half + 3, 0:C_N],
                                   ACT.Copy).then_inc(evac, 1)
                    if not last:
                        split_high(j + (KC // 2 + 2), half)
                act.wait_ge(conv, j * 6 + 3)
                act.activation(acc[0], acc[0], ACT.Silu).then_inc(silu, 1)
                down_high(j, first)
                act.wait_ge(prod, j + 1)
                act.activation(ah[s][:, :], acc[0], ACT.Copy).then_inc(act_hi, 1)

            hidden(0, 0, first=True)
            hidden(1, 1)
            with act.Fori(1, FT // 2 - 1) as i:
                hidden(i * 2, 0)
                hidden(i * 2 + 1, 1)
            hidden(FT - 2, 0)
            hidden(FT - 1, 1, last=True)
            act.preload_act_table_set("natural_log_exp_and_others")
            for t in range(SEQ // P):
                act.wait_ge(turned, t + 1)
                if t >= 2:
                    act.wait_ge(row_sum, t - 1)
                else:
                    act.wait_ge(prod, FT)
                act.activation(junk[t % 2].rearrange("p (b c) -> p b c", b=2),
                               psum[:, 2 * (t % 4):2 * (t % 4) + 2, :], ACT.Square,
                               accum_out=rsum[:, t:t + 1]).then_inc(row_sum, 1)
                act.wait_ge(row_sum, t + 1)
                act.activation(rln[:, t:t + 1], rsum[:, t:t + 1], ACT.Ln, bias=eps, scale=1.0 / D).then_inc(row_ln, 1)
                act.wait_ge(row_ln, t + 1)
                act.activation(rnorm[:, t:t + 1], rln[:, t:t + 1], ACT.Exp, scale=-0.5).then_inc(row_norm, 1)

        @block.vector
        def _(dve):
            def split_low(count, s):
                dve.wait_ge(w_hi, count)
                dve.tensor_tensor(wl[s][:, :, :], wraw[s][:, :, :], wh[s][:, :, :].bitcast(F32),
                                  ALU.subtract).then_inc(w_lo, 1)

            def y_low(k):
                dve.wait_ge(y_hi, k + 1)
                dve.tensor_tensor(xl[:, k, :], y[:, k, C_COL:T], xh[:, k, :].bitcast(F32),
                                  ALU.subtract).then_inc(y_split, 1)

            split_low(1, 0)
            y_low(0)
            split_low(2, 1)
            for k in range(1, KC):
                y_low(k)
            dve.wait_ge(h_in, 16)

            def add_square(m):
                if m:
                    dve.wait_ge(squared, m + 1)
                    dve.wait_ge(summed, m)
                    dve.tensor_tensor(ssq, ssq, sq[m % 2], ALU.add).then_inc(summed, 1)
                else:
                    dve.wait_ge(squared, 1)
                    dve.memset(rsum[:, :], 0.0).then_inc(summed, 1)

            for m in range(KC):
                dve.wait_ge(mm_done, m + 1)
                dve.tensor_tensor(thirds(h[:, m, :]), psum[:, 3 * (m % 2):3 * (m % 2) + 3, 0:C_N],
                                  thirds(h[:, m, :]), ALU.add).then_inc(h_added, 1)
                split_low(m + 3, m % 2)
                if m:
                    add_square(m - 1)
            add_square(KC - 1)
            dve.wait_ge(rms_ready, 1)
            dve.wait_ge(tables, 48)

            def low_part(k):
                dve.wait_ge(normed, k + 1)
                dve.wait_ge(x_hi, k + 1)
                dve.tensor_tensor(xl[:, k, :], xn[k % 2], xh[:, k, :].bitcast(F32), ALU.subtract).then_inc(x_split, 1)

            for k in range(KC):
                if k >= 2:
                    dve.wait_ge(x_split, k - 1)
                dve.scalar_tensor_tensor(out=xn[k % 2], in0=h[:, k, :], scalar=par[:, PAR_N2 + k:PAR_N2 + k + 1],
                                         in1=rbc, op0=ALU.mult, op1=ALU.mult).then_inc(normed, 1)
                if k:
                    low_part(k - 1)
            low_part(KC - 1)

            def taps(j, half):
                def weight(at):
                    return par[:, bass.ds(j + (at + FT * half), 1)]

                dve.wait_ge(evac, j * 2 + (half + 1))
                dve.tensor_scalar(acc[half], raw[half][:, 0:SEQ], weight(PAR_FCONV), weight(PAR_FB), ALU.mult,
                                  ALU.add).then_inc(conv, 1)
                for k in range(1, FCONV):
                    dve.wait_ge(conv, j * 6 + (3 * half + k))
                    dve.scalar_tensor_tensor(out=acc[half], in0=raw[half][:, k:k + SEQ],
                                             scalar=weight(PAR_FCONV + 2 * FT * k), in1=acc[half], op0=ALU.mult,
                                             op1=ALU.add).then_inc(conv, 1)

            def add_down(j, first=False):
                for n in range(HALVES):
                    at = h[:, n // 2, 2 + (n % 2) * 512:2 + (n % 2) * 512 + 512]
                    dve.wait_ge(down, j * HALVES + (n + 1))
                    if n == 0 and not first:
                        dve.wait_ge(added, j * HALVES)
                    dve.tensor_tensor(at, psum[:, ADD_BANKS[n % 5], :], at, ALU.add).then_inc(added, 1)

            def hidden(j, s, first=False, last=False, add=True):
                if not first:
                    dve.wait_ge(act_lo, j)
                taps(j, 0)
                if not last:
                    split_low(j * 2 + (KC + 3), 0)
                if not first:
                    add_down(j - 1, isinstance(j, int) and j == 1)
                taps(j, 1)
                if not last:
                    split_low(j * 2 + (KC + 4), 1)
                dve.wait_ge(silu, j + 1)
                dve.wait_ge(conv, j * 6 + 6)
                dve.tensor_tensor(acc[0], acc[0], acc[1], ALU.mult).then_inc(prod, 1)
                dve.wait_ge(d_hi, j + 1)
                dve.tensor_tensor(dl[:, :], draw[:, :], dh[:, :].bitcast(F32), ALU.subtract).then_inc(d_lo, 1)
                dve.wait_ge(prod, j + 1)
                dve.wait_ge(act_hi, j + 1)
                dve.tensor_tensor(al[s][:, :], acc[0], ah[s][:, :].bitcast(F32), ALU.subtract).then_inc(act_lo, 1)

            hidden(0, 0, first=True)
            hidden(1, 1)
            with dve.Fori(1, FT // 2 - 1) as i:
                hidden(i * 2, 0)
                hidden(i * 2 + 1, 1)
            hidden(FT - 2, 0)
            hidden(FT - 1, 1, last=True)
            add_down(FT - 1)
            for t in range(SEQ // P):
                dve.wait_ge(row_norm, t + 1)
                if t >= 2:
                    dve.wait_ge(row_stored[t % 2], 16 * (t // 2))
                dve.scalar_tensor_tensor(out=rows[t % 2].rearrange("p (b c) -> p b c", b=2),
                                         in0=psum[:, 2 * (t % 4):2 * (t % 4) + 2, :], scalar=rnorm[:, t:t + 1],
                                         in1=gf[:, :].rearrange("p (b c) -> p b c", b=2), op0=ALU.mult,
                                         op1=ALU.mult).then_inc(row_out, 1)


INPUTS = ("x", "meta", "norm1", "w_in", "gdn_conv_w", "gdn_a_log", "gdn_dt_bias", "gdn_norm", "w_out", "norm2",
          "w_ffn_up", "ffn_conv_w", "ffn_conv_b", "w_ffn_down", "norm_f")


def layer(nc, io, out):
    sc = {
        "mix": nc.dram_tensor("mix_scratch", (S_N, P, T), F32, kind="Internal").ap(),
        "hT": nc.dram_tensor("hT_scratch", (P, KC, T), F32, kind="Internal").ap(),
        "gates": nc.dram_tensor("gates_scratch", (P, NCH, 2 * GH), F32, kind="Internal").ap(),
        "par": nc.dram_tensor("par_scratch", (P, PAR_W), F32, kind="Internal").ap(),
    }
    input_phase(nc, io, sc)
    with nc.sbuf_tensor("y", [P, KC, T], F32) as y:
        mixer_phase(nc, io, sc, y)
        output_phase(nc, io, sc, y, out)


def kernel(**inputs):
    import concourse.bacc as _bacc
    from concourse.bass_utils import run_bass_kernel_spmd as _run

    nc = _bacc.Bacc("TRN2", target_bir_lowering=False, num_devices=1)
    consts, rope = shape_constants()
    arrays = {f"in_{n}": np.ascontiguousarray(inputs[n]) for n in INPUTS}
    arrays["in_cst"], arrays["in_rope"] = consts, np.ascontiguousarray(rope)
    io = {n[3:]: nc.dram_tensor(n, a.shape, mybir.dt.from_np(a.dtype), kind="ExternalInput").ap()
          for n, a in arrays.items()}
    out = nc.dram_tensor("out_0", (1, SEQ, D), F32, kind="ExternalOutput").ap()
    layer(nc, io, out)
    r = _run(nc, [arrays], core_ids=[0])
    return r.results[0]["out_0"]
```

```python
import math
from contextlib import ExitStack

import numpy as np

import concourse.bass as bass
from concourse import mybir

F32 = mybir.dt.float32
F32R = mybir.dt.float32r
ACT = mybir.ActivationFunctionType
ALU = mybir.AluOpType
AX = mybir.AxisListType

P = 128
D = 1024
KC = D // P
SEQ = 1024
META = 16
CH = 128
NCH = 9
T = NCH * CH
PAD = T - META - SEQ
GH = 8
RH = 4
HALF = 128
D_FF = 2816
FT = D_FF // P
GCONV = 4
FCONV = 3
EPS = 1e-6
SLOTS = 2

A_COL = PAD - 4
A_N = (T - A_COL) // 3
C_COL = PAD + META - (FCONV - 1)
C_W = T - C_COL
C_N = C_W // 3
X0 = PAD + META

Q0, K0, V0, Z0 = 0, 1024, 2048, 3072
GA0 = 4096
RQ0 = GA0 + 2 * GH
RK0, RV0, RG0, GATEA0, GATEB0 = (RQ0 + D * n for n in range(1, 6))

PAR_GCONV = 0
PAR_N1 = PAR_GCONV + GCONV * 24
PAR_N2 = PAR_N1 + KC
PAR_GN = PAR_N2 + KC
PAR_FCONV = PAR_GN + 1
PAR_FB = PAR_FCONV + FCONV * 2 * FT
PAR_W = PAR_FB + 2 * FT

C_ID = 0
C_ONES = C_ID + P
C_TRIU = C_ONES + P
C_UPTO = C_TRIU + P
C_BELOW = C_UPTO + P
C_LEVEL = C_BELOW + P
NLEVEL = 7
C_RDEC = C_LEVEL + NLEVEL * 64
C_RROW = C_RDEC + RH * CH
C_RCOL = C_RROW + RH * CH
C_EPS = C_RCOL + RH
C_LNQ = C_EPS + 1
C_W_ALL = C_LNQ + 1

S_Q, S_K, S_V = 0, 8, 16
S_ZA, S_ZB = 24, 32
S_RQ, S_RK, S_RV = 40, 48, 56
S_N = 64


def shape_constants():
    c = np.zeros((P, C_W_ALL), np.float64)
    i = np.arange(P)
    c[:, C_ID:C_ID + P] = np.eye(P)
    c[:, C_ONES:C_ONES + P] = 1
    upto = i[:, None] <= i[None, :]
    c[:, C_TRIU:C_TRIU + P] = upto
    c[:, C_UPTO:C_UPTO + P] = np.where(upto, 0, -1e30)
    c[:, C_BELOW:C_BELOW + P] = np.where(i[None, :] < i[:, None], 0, 1e30)
    for lv in range(NLEVEL):
        b = 1 << lv
        odd = np.array([m for m in range(P) if (m // b) % 2])
        c[:, C_LEVEL + 64 * lv:C_LEVEL + 64 * lv + 64] = -1.0 * (i[:, None] // b == odd[None, :] // b - 1)
    lg = np.log(1.0 - 2.0 ** (-5.0 - np.arange(RH)))
    scale = (2 * HALF) ** -0.5
    for h in range(RH):
        dec = np.where(upto, np.exp(np.minimum(i[None, :] - i[:, None], CH) * lg[h]), 0) * scale
        c[:, C_RDEC + CH * h:C_RDEC + CH * h + CH] = dec
        c[:, C_RROW + CH * h:C_RROW + CH * h + CH] = np.exp((i[None, :] + 1) * lg[h])
        c[:, C_RCOL + h] = np.exp((CH - 1 - i) * lg[h]) * scale
    c[:, C_EPS] = EPS
    c[:, C_LNQ] = math.log(P ** -0.5)
    half = HALF
    inv = (1.0 / (np.float32(10000.0) ** (np.arange(half, dtype=np.float32) / np.float32(half)))).astype(np.float32)
    pos = np.arange(META + SEQ, dtype=np.float32)
    ang = (pos[None, :] * inv[:, None]).astype(np.float32).astype(np.float64)
    rope = np.stack([np.cos(ang), np.sin(ang)], 1)
    return c.astype(np.float32), rope.astype(np.float32)


def project_block(pe, psum, bank, wh, wl, xh, xl, k, col, n):
    for part, (w, x) in enumerate(((wh, xh), (wh, xl), (wl, xh))):
        for j in range(3):
            mm = pe.matmul(psum[:, bank + j, 0:n], w[:, k, :], x[:, k, col + n * j:col + n * j + n],
                           start=(k == 0 and part == 0), stop=(k == KC - 1 and part == 2))
    return mm


def project(pe, psum, bank, wh, wl, xh, xl, col, n, block_ready=None):
    for k in range(KC):
        if block_ready is not None:
            pe.wait_ge(block_ready, k + 1)
        mm = project_block(pe, psum, bank, wh, wl, xh, xl, k, col, n)
    return mm


def project_two(pe, psum, wh, wl, xh, xl, col, n, block_ready, done):
    for k in range(KC):
        pe.wait_ge(block_ready, k + 1)
        for s in range(SLOTS):
            mm = project_block(pe, psum, 3 * s, wh[s], wl[s], xh, xl, k, col, n)
            if k == KC - 1:
                mm.then_inc(done, 1)


def input_phase(nc, io, sc):
    with ExitStack() as ctx:
        def sb(name, shape, dt=F32):
            return ctx.enter_context(nc.sbuf_tensor(name, shape, dt))

        def sem(name):
            return ctx.enter_context(nc.semaphore(name))

        psum = ctx.enter_context(nc.psum_tensor("a_psum", [P, 8, 512], F32))
        cst = sb("a_cst", [P, C_W_ALL])
        rope = sb("rope", [P, 2, META + SEQ])
        prow = sb("param_rows", [P, 3, P])
        par = sb("a_par", [P, PAR_W])
        arow = sb("decay_rows", [P, 2, GH])
        xt = sb("x_tokens", [P, SLOTS, D])
        hT = sb("hT", [P, KC, T])
        sq = sb("squares", [P, SLOTS, KC, CH])
        ssq = sb("square_sums", [P, T])
        rbc = sb("rms_rows", [P, T])
        xn = sb("normed_block", [P, SLOTS, T])
        xh = sb("xh", [P, KC, T], F32R)
        xl = sb("xl", [P, KC, T], F32R)
        wraw = [sb(f"w_raw{s}", [P, KC, P]) for s in range(SLOTS)]
        wh = [sb(f"w_hi{s}", [P, KC, P], F32R) for s in range(SLOTS)]
        wl = [sb(f"w_lo{s}", [P, KC, P], F32R) for s in range(SLOTS)]
        raw = [xt[:, 0:2, :].rearrange("p a b -> p (a b)")[:, 0:3 * A_N],
               sq[:, 0:2, :, :].rearrange("p a b c -> p (a b c)")[:, 0:3 * A_N]]
        work = [ssq[:, :], rbc[:, :]]
        stage = [xn[:, 0, :], xn[:, 1, :]]

        abT = sb("gates_T", [2 * GH, T])
        gates = sb("gates", [P, NCH, 2 * GH])
        gtmp = sb("gates_work", [P, NCH, 2 * GH])
        gabs = sb("gates_abs", [P, NCH, GH])
        rate = sb("decay_rate", [P, GH])
        AB_STEPS = 12

        consts_in = sem("consts_in")
        params_in = sem("params_in")
        x_slot = [xt[:, 0, :], xt[:, 1, :], xn[:, 0, 0:D], xn[:, 1, 0:D]]
        x_in = [sem(f"x_in{s}") for s in range(4)]
        rope_in = sem("rope_in")
        pad_zero = sem("pad_zero")
        turned = sem("turned")
        par_out = sem("par_out")
        hT_out = sem("hT_out")
        squared = sem("squared")
        summed = sem("summed")
        ss_ready = sem("ss_ready")
        ln_done = sem("ln_done")
        rms_ready = sem("rms_ready")
        normed = sem("normed")
        x_hi = sem("x_hi")
        x_split = sem("x_split")
        h_stored = sem("h_stored")
        w_loaded = [sem(f"w_loaded{s}") for s in range(SLOTS)]
        w_hi = sem("w_hi")
        w_lo = sem("w_lo")
        mm_done = sem("mm_done")
        evac = sem("evac")
        taps = sem("taps")
        conv_done = sem("conv_done")
        activated = sem("activated")
        gate_mul = sem("gate_mul")
        gated = sem("gated")
        rot_mul = sem("rot_mul")
        rotated = sem("rotated")
        stored = [sem(f"stored{s}") for s in range(SLOTS)]
        ab_raw = sem("ab_raw")
        ab_turned = sem("ab_turned")
        ab_step = sem("ab_step")
        ab_stored = sem("ab_stored")
        block = ctx.enter_context(nc.Block())

        w_in = io["w_in"][0].rearrange("(k p) n -> p k n", p=P)
        NT = 80
        CONV, ZA, ZB, ROT, RV = (
            (0, 12, Q0, 256, Q0 + P, 256),
            (12, 8, Z0, P, GATEA0, P),
            (20, 8, RG0, P, GATEB0, P),
            (28, 8, RQ0, 256, RQ0 + P, 256),
            (36, 4, RV0, 256, RV0 + P, 256))
        SEGMENTS = (CONV, ZA, ZB, ROT, RV)

        @block.sync
        def _(sp):
            sp.dma_start(cst[:, :], io["cst"]).then_inc(consts_in, 16)
            sp.dma_start(xt[PAD:P, 0, :], io["meta"]).then_inc(x_in[0], 16)
            for c in range(1, 4):
                sp.dma_start(x_slot[c], io["x"][0, (c - 1) * P:c * P, :]).then_inc(x_in[c], 16)
            g = prow[0:96, 0, :]
            sp.dma_start(g, io["gdn_conv_w"][0].rearrange("j (t p) -> (j t) p", p=P)).then_inc(params_in, 16)
            sp.dma_start(prow[96:104, 0, :], io["norm1"][0].rearrange("(t p) -> t p", p=P)).then_inc(params_in, 16)
            sp.dma_start(prow[104:112, 0, :], io["norm2"][0].rearrange("(t p) -> t p", p=P)).then_inc(params_in, 16)
            sp.dma_start(prow[112:113, 0, :], io["gdn_norm"]).then_inc(params_in, 16)
            fw = io["ffn_conv_w"][0].rearrange("j (t p) -> j t p", p=P)
            fb = io["ffn_conv_b"][0].rearrange("(t p) -> t p", p=P)
            sp.dma_start(prow[0:44, 1, :], fw[0]).then_inc(params_in, 16)
            sp.dma_start(prow[44:88, 1, :], fw[1]).then_inc(params_in, 16)
            sp.dma_start(prow[0:44, 2, :], fw[2]).then_inc(params_in, 16)
            sp.dma_start(prow[44:88, 2, :], fb).then_inc(params_in, 16)
            sp.dma_start(arow[:, 0, :], io["gdn_a_log"].broadcast_to((P, GH))).then_inc(params_in, 16)
            sp.dma_start(arow[:, 1, :], io["gdn_dt_bias"].broadcast_to((P, GH))).then_inc(params_in, 16)
            for c in range(4, NCH):
                sp.wait_ge(turned, c - 3)
                sp.dma_start(x_slot[c % 4], io["x"][0, (c - 1) * P:c * P, :]).then_inc(x_in[c % 4], 16)
            for s in range(SLOTS):
                sp.dma_start(wraw[s][:, :, :], w_in[:, :, Q0 + P * s:Q0 + P * s + P]).then_inc(w_loaded[s], 16)
            sp.dma_start(rope[:, :, :], io["rope"]).then_inc(rope_in, 16)
            sp.wait_ge(hT_out, NCH)
            sp.dma_start(sc["hT"], hT[:, :, :]).then_inc(h_stored, 16)
            mix = sc["mix"].rearrange("s p c -> p s c")
            for s in range(SLOTS):
                sp.sem_inc(stored[s], 16)

            def load(pair, starts):
                for s in range(SLOTS):
                    sp.wait_ge(w_lo, pair * 2 + (s + 1))
                    sp.dma_start(wraw[s][:, :, :], w_in[:, :, bass.ds(starts[s], P)]).then_inc(w_loaded[s], 16)

            def store(s, tile, done, count):
                sp.wait_ge(done, count)
                sp.dma_start(mix[:, bass.ds(tile, 1), :],
                             stage[s].rearrange("p (o c) -> p o c", o=1)).then_inc(stored[s], 16)

            def store_pair(seg, i):
                if seg is CONV:
                    for s in range(SLOTS):
                        store(s, i * 2 + s, activated, i * 2 + (s + 3))
                elif seg is ZA or seg is ZB:
                    g = i + (seg[0] - ZA[0])
                    store(0, g + S_ZA, gated, g + 2)
                elif seg is ROT:
                    store(0, i * 2 + S_RQ, rot_mul, i * 5 + 3)
                    store(1, i * 2 + (S_RQ + 1), rotated, i + 2)
                else:
                    for s in range(SLOTS):
                        store(s, i * 2 + (S_RV + s), evac, i * 2 + (2 * RV[0] + s + 3))

            for n, seg in enumerate(SEGMENTS):
                first, pairs, a0, da, b0, db = seg
                with sp.Fori(0, pairs - 1) as i:
                    load(i + first, (i * da + (a0 + da), i * db + (b0 + db)))
                    store_pair(seg, i)
                if n + 1 < len(SEGMENTS):
                    load(first + pairs - 1, (SEGMENTS[n + 1][2], SEGMENTS[n + 1][4]))
                    store_pair(seg, pairs - 1)
            sp.wait_ge(w_lo, NT - 1)
            sp.dma_start(wraw[0][:, :, 0:2 * GH], w_in[:, :, GA0:GA0 + 2 * GH]).then_inc(w_loaded[0], 16)
            store_pair(RV, RV[1] - 1)
            for s in range(SLOTS):
                sp.wait_ge(stored[s], 16 * (41 - 16 * s))
            sp.wait_ge(h_stored, 16)
            sp.wait_ge(ab_step, AB_STEPS)
            sp.dma_start(sc["gates"], gates[:, :, :]).then_inc(ab_stored, 16)
            sp.dma_start(sc["par"], par[:, :]).then_inc(ab_stored, 16)
            sp.wait_ge(ab_stored, 32)

        @block.tensor
        def _(pe):
            pe.wait_ge(consts_in, 16)
            ident = cst[:, C_ID:C_ID + P]
            for c in range(NCH):
                s = c % 2
                pe.wait_ge(x_in[c % 4], 16 * (c // 4 + 1))
                if c == 0:
                    pe.wait_ge(pad_zero, 1)
                if c >= 2:
                    pe.wait_ge(hT_out, c - 1)
                for k in range(KC):
                    mm = pe.transpose(psum[:, 2 * s + k // 4, (k % 4) * P:(k % 4) * P + P],
                                      x_slot[c % 4][:, k * P:k * P + P], ident)
                mm.then_inc(turned, 1)
            pe.wait_ge(params_in, 160)
            for g, rows in enumerate((113, 88, 88)):
                mm = pe.transpose(psum[:, 7, g * P:g * P + rows], prow[0:rows, g, :], ident[0:rows, 0:rows])
            mm.then_inc(turned, 1)
            pe.wait_ge(summed, NCH)
            for j in range(3):
                mm = pe.matmul(psum[:, 4 + j, 0:T // 3], cst[:, C_ONES:C_ONES + P],
                               ssq[:, j * (T // 3):(j + 1) * (T // 3)], start=True, stop=True)
            mm.then_inc(ss_ready, 1)

            def tile(p, s):
                pe.wait_ge(w_lo, p + 1)
                pe.wait_ge(evac, p + 1)
                project(pe, psum, 3 * s, wh[s], wl[s], xh, xl, A_COL, A_N).then_inc(mm_done, 1)

            pe.wait_ge(rms_ready, 1)
            pe.wait_ge(w_lo, SLOTS)
            project_two(pe, psum, wh, wl, xh, xl, A_COL, A_N, x_split, mm_done)
            with pe.Fori(1, NT // 2) as i:
                for s in range(SLOTS):
                    tile(i * 2 + s, s)
            tile(NT, 0)
            pe.wait_ge(ab_raw, 2)
            for c in range(NCH):
                mm = pe.transpose(psum[:, 6, c * 2 * GH:(c + 1) * 2 * GH],
                                  abT[:, c * CH:c * CH + CH], ident[0:2 * GH, 0:2 * GH])
            mm.then_inc(ab_turned, 1)

        @block.scalar
        def _(act):
            act.sem_inc(evac, SLOTS)
            act.sem_inc(activated, SLOTS)
            act.preload_act_table_set("natural_log_exp_and_others")
            act.wait_ge(consts_in, 16)
            for c in range(NCH):
                s = c % 2
                act.wait_ge(turned, c + 1)
                act.activation(hT[:, :, c * CH:c * CH + CH], psum[:, 2 * s:2 * s + 2, :].rearrange(
                    "p b (k c) -> p (b k) c", c=CH), ACT.Copy).then_inc(hT_out, 1)
                act.wait_ge(hT_out, c + 1)
                if c >= 2:
                    act.wait_ge(summed, c - 1)
                act.activation(sq[:, s, :, :], hT[:, :, c * CH:c * CH + CH], ACT.Square).then_inc(squared, 1)
            for s in range(SLOTS):
                act.wait_ge(w_loaded[s], 16)
                act.activation(wh[s][:, :, :], wraw[s][:, :, :], ACT.Copy).then_inc(w_hi, 1)
            act.wait_ge(ss_ready, 1)
            act.activation(rbc[:, :].rearrange("p (b c) -> p b c", b=3), psum[:, 4:7, 0:T // 3], ACT.Ln,
                           bias=cst[:, C_EPS:C_EPS + 1], scale=1.0 / D).then_inc(ln_done, 1)
            act.wait_ge(ln_done, 1)
            act.activation(rbc[:, :], rbc[:, :], ACT.Exp, scale=-0.5).then_inc(rms_ready, 1)
            for k in range(KC):
                act.wait_ge(normed, k + 1)
                act.activation(xh[:, k, :], xn[:, k % 2, :], ACT.Copy).then_inc(x_hi, 1)

            def banks(s):
                return psum[:, 3 * s:3 * s + 3, 0:A_N]

            def flat(buf):
                return buf[:, 0:3 * A_N].rearrange("p (b c) -> p b c", b=3)

            def split_next(pair, s):
                act.wait_ge(w_loaded[s], pair * 16 + 32)
                act.activation(wh[s][:, :, :], wraw[s][:, :, :], ACT.Copy).then_inc(w_hi, 1)

            act.wait_ge(x_split, KC)
            act.preload_act_table_set("silu_and_others")
            with act.Fori(0, CONV[1]) as i:
                for s in range(SLOTS):
                    act.wait_ge(mm_done, i * 2 + s + 1)
                    act.wait_ge(conv_done, i * 2 + s + 1)
                    act.activation(flat(raw[s]), banks(s), ACT.Copy).then_inc(evac, 1)
                    split_next(i, s)
                    act.wait_ge(conv_done, i * 2 + s + 3)
                    act.wait_ge(stored[s], i * 16 + 16)
                    act.activation(stage[s][:, PAD:T], work[s][:, 0:T - PAD], ACT.Silu).then_inc(activated, 1)
            act.preload_act_table_set("sigmoid_and_others")
            act.wait_ge(activated, 24 + SLOTS)
            with act.Fori(0, ZA[1] + ZB[1]) as i:
                act.wait_ge(mm_done, i * 2 + (2 * ZA[0] + 1))
                act.wait_ge(gated, i + 1)
                act.activation(flat(raw[0]), banks(0), ACT.Copy)
                act.activation(flat(work[0]), banks(0), ACT.Sigmoid).then_inc(evac, 1)
                split_next(i + ZA[0], 0)
                act.wait_ge(mm_done, i * 2 + (2 * ZA[0] + 2))
                act.activation(flat(work[1]), banks(1), ACT.Sigmoid).then_inc(evac, 1)
                split_next(i + ZA[0], 1)
            act.wait_ge(gated, 17)
            with act.Fori(0, ROT[1]) as i:
                for s in range(SLOTS):
                    act.wait_ge(mm_done, i * 2 + (2 * ROT[0] + s + 1))
                    act.wait_ge(rotated, i + 1)
                    act.activation(flat(raw[s]), banks(s), ACT.Copy).then_inc(evac, 1)
                    split_next(i + ROT[0], s)

            def values(i, s, more):
                act.wait_ge(mm_done, i * 2 + (2 * RV[0] + s + 1))
                act.wait_ge(stored[s], i * 16 + 16 * (RV[0] - 16 * s + 1))
                act.activation(flat(stage[s][:, A_COL:T]), banks(s), ACT.Copy).then_inc(evac, 1)
                if more:
                    split_next(i + RV[0], s)

            act.wait_ge(rotated, 9)
            with act.Fori(0, RV[1] - 1) as i:
                for s in range(SLOTS):
                    values(i, s, True)
            values(RV[1] - 1, 0, True)
            values(RV[1] - 1, 1, False)
            act.preload_act_table_set("natural_log_exp_and_others")
            act.wait_ge(mm_done, NT + 1)
            act.activation(abT[:, A_COL:T].rearrange("p (b c) -> p b c", b=3), psum[0:2 * GH, 0:3, 0:A_N],
                           ACT.Copy).then_inc(ab_raw, 1)
            act.wait_ge(ab_step, 1)
            turned_gates = psum[:, 6, 0:NCH * 2 * GH].rearrange("p (c g) -> p c g", c=NCH)
            act.activation(gtmp[:, :, GH:2 * GH], turned_gates[:, :, GH:2 * GH], ACT.Exp,
                           scale=-1.0).then_inc(ab_step, 1)
            act.activation(gabs[:, :, :], gtmp[:, :, 0:GH], ACT.Abs).then_inc(ab_step, 1)
            act.wait_ge(ab_step, 3)
            act.activation(gabs[:, :, :], gabs[:, :, :], ACT.Exp, scale=-1.0).then_inc(ab_step, 1)
            act.wait_ge(ab_step, 4)
            act.activation(gabs[:, :, :], gabs[:, :, :], ACT.Ln, bias=1.0).then_inc(ab_step, 1)
            act.activation(rate[:, :], arow[:, 0, :], ACT.Exp).then_inc(ab_step, 1)

        @block.vector
        def _(dve):
            dve.sem_inc(conv_done, SLOTS)
            dve.sem_inc(gated, 1)
            dve.sem_inc(rotated, 1)
            dve.memset(xt[0:PAD, 0, :], 0.0).then_inc(pad_zero, 1)
            for c in range(NCH):
                dve.wait_ge(squared, c + 1)
                dve.tensor_reduce(ssq[:, c * CH:c * CH + CH], sq[:, c % 2, :, :].rearrange("p k c -> p c k"),
                                  AX.X, ALU.add).then_inc(summed, 1)
            dve.wait_ge(turned, NCH + 1)
            for g, (at, n) in enumerate(((0, PAR_FCONV), (PAR_FCONV, 88), (PAR_FCONV + 88, 88))):
                dve.tensor_copy(par[:, at:at + n], psum[:, 7, g * P:g * P + n]).then_inc(par_out, 1)
            for s in range(SLOTS):
                dve.wait_ge(w_hi, s + 1)
                dve.tensor_tensor(wl[s][:, :, :], wraw[s][:, :, :], wh[s][:, :, :].bitcast(F32),
                                  ALU.subtract).then_inc(w_lo, 1)
            dve.wait_ge(par_out, 3)
            dve.wait_ge(rms_ready, 1)

            def low_part(k):
                dve.wait_ge(normed, k + 1)
                dve.wait_ge(x_hi, k + 1)
                dve.tensor_tensor(xl[:, k, :], xn[:, k % 2, :], xh[:, k, :].bitcast(F32),
                                  ALU.subtract).then_inc(x_split, 1)

            for k in range(KC):
                if k >= 2:
                    dve.wait_ge(x_split, k - 1)
                dve.scalar_tensor_tensor(out=xn[:, k % 2, :], in0=hT[:, k, :], scalar=par[:, PAR_N1 + k:PAR_N1 + k + 1],
                                         in1=rbc[:, :], op0=ALU.mult, op1=ALU.mult).then_inc(normed, 1)
                if k:
                    low_part(k - 1)
            low_part(KC - 1)

            def split_low(tile, s):
                dve.wait_ge(w_hi, tile + 1)
                dve.tensor_tensor(wl[s][:, :, :], wraw[s][:, :, :], wh[s][:, :, :].bitcast(F32),
                                  ALU.subtract).then_inc(w_lo, 1)

            N = T - PAD
            def convolve(i, first=False):
                for s in range(SLOTS):
                    acc = work[s][:, 0:N]
                    if first:
                        split_low(i * 2 + (s + 2), s)
                    dve.wait_ge(evac, i * 2 + s + 3)
                    dve.wait_ge(activated, i * 2 + s + 1)

                    def tap(j):
                        return raw[s][:, 1 + j:1 + j + N], par[:, bass.ds(i * 2 + (s + PAR_GCONV + 24 * j), 1)]

                    x, w = tap(0)
                    dve.tensor_scalar(acc, x, w, None, ALU.mult).then_inc(taps, 1)
                    for j in range(1, GCONV):
                        x, w = tap(j)
                        dve.wait_ge(taps, i * 6 + (3 * s + j))
                        dve.scalar_tensor_tensor(out=acc, in0=x, scalar=w, in1=acc, op0=ALU.mult,
                                                 op1=ALU.add).then_inc(taps if j < 3 else conv_done, 1)
                    if not first:
                        split_low(i * 2 + (s + 2), s)

            convolve(0, first=True)
            with dve.Fori(1, CONV[1]) as i:
                convolve(i)

            def gate(i, pair0, zout, norm):
                dve.wait_ge(evac, i * 2 + (2 * pair0 + 3))
                dve.tensor_tensor(work[0][:, 0:3 * A_N], work[0][:, 0:3 * A_N], raw[0][:, 0:3 * A_N],
                                  ALU.mult).then_inc(gate_mul, 1)
                split_low(i * 2 + (2 * pair0 + 2), 0)
                dve.wait_ge(evac, i * 2 + (2 * pair0 + 4))
                dve.wait_ge(gate_mul, i + (pair0 - ZA[0] + 1))
                dve.wait_ge(stored[0], i * 16 + (16 * pair0 + 16))
                out = stage[0][:, A_COL:T]
                if norm:
                    dve.scalar_tensor_tensor(out=out, in0=work[0][:, 0:3 * A_N], scalar=par[:, PAR_GN:PAR_GN + 1],
                                             in1=work[1][:, 0:3 * A_N], op0=ALU.mult,
                                             op1=ALU.mult).then_inc(gated, 1)
                else:
                    dve.tensor_tensor(out, work[0][:, 0:3 * A_N], work[1][:, 0:3 * A_N],
                                      ALU.mult).then_inc(gated, 1)
                split_low(i * 2 + (2 * pair0 + 3), 1)

            with dve.Fori(0, ZA[1]) as i:
                gate(i, ZA[0], S_ZA, True)
            with dve.Fori(0, ZB[1]) as i:
                gate(i, ZB[0], S_ZB, False)
            cos, sin = rope[:, 0, :], rope[:, 1, :]
            dve.wait_ge(rope_in, 16)
            with dve.Fori(0, ROT[1]) as i:
                x1, x2 = raw[0][:, 4:4 + N], raw[1][:, 4:4 + N]
                a, b = work[0][:, 0:N], work[1][:, 0:N]
                split_low(i * 2 + (2 * ROT[0] + 2), 0)
                dve.wait_ge(evac, i * 2 + (2 * ROT[0] + 4))
                dve.tensor_tensor(a, x1, cos, ALU.mult).then_inc(rot_mul, 1)
                dve.tensor_tensor(b, x2, sin, ALU.mult).then_inc(rot_mul, 1)
                dve.wait_ge(rot_mul, i * 5 + 2)
                dve.wait_ge(stored[0], i * 16 + 16 * (ROT[0] + 1))
                dve.tensor_tensor(stage[0][:, PAD:T], a, b, ALU.subtract).then_inc(rot_mul, 1)
                split_low(i * 2 + (2 * ROT[0] + 3), 1)
                dve.wait_ge(rot_mul, i * 5 + 3)
                dve.tensor_tensor(a, x2, cos, ALU.mult).then_inc(rot_mul, 1)
                dve.tensor_tensor(b, x1, sin, ALU.mult).then_inc(rot_mul, 1)
                dve.wait_ge(rot_mul, i * 5 + 5)
                dve.wait_ge(stored[1], i * 16 + 16 * (ROT[0] - 15))
                dve.tensor_tensor(stage[1][:, PAD:T], a, b, ALU.add).then_inc(rotated, 1)
            with dve.Fori(0, RV[1] - 1) as i:
                for s in range(SLOTS):
                    split_low(i * 2 + (2 * RV[0] + s + 2), s)
            split_low(NT, 0)
            turned_gates = psum[:, 6, 0:NCH * 2 * GH].rearrange("p (c g) -> p c g", c=NCH)
            dve.wait_ge(ab_turned, 1)
            dve.tensor_tensor(gtmp[:, :, 0:GH], turned_gates[:, :, 0:GH],
                              arow[:, 1:2, :].broadcast_to((P, NCH, GH)), ALU.add).then_inc(ab_step, 1)
            dve.wait_ge(ab_step, 6)
            dve.tensor_scalar(gtmp[:, :, GH:2 * GH], gtmp[:, :, GH:2 * GH], 1.0, None, ALU.add).then_inc(ab_step, 1)
            dve.scalar_tensor_tensor(out=gabs[:, :, :], in0=gtmp[:, :, 0:GH], scalar=0.0, in1=gabs[:, :, :],
                                     op0=ALU.max, op1=ALU.add).then_inc(ab_step, 1)
            dve.wait_ge(ab_step, 8)
            dve.reciprocal(gates[:, :, GH:2 * GH], gtmp[:, :, GH:2 * GH]).then_inc(ab_step, 1)
            dve.tensor_tensor(gtmp[:, :, 0:GH], gabs[:, :, :],
                              rate[:, :].rearrange("p (a g) -> p a g", a=1).broadcast_to((P, NCH, GH)),
                              ALU.mult).then_inc(ab_step, 1)
            dve.wait_ge(ab_step, 10)
            dve.tensor_scalar(gates[:, :, 0:GH], gtmp[:, :, 0:GH], -1.0, None, ALU.mult).then_inc(ab_step, 1)
            dve.wait_ge(ab_step, 11)
            dve.memset(gates[0:PAD, 0, 0:GH], 0.0).then_inc(ab_step, 1)

        @block.gpsimd
        def _(pool):
            pool.memset(abT[:, 0:A_COL], 0.0).then_inc(ab_raw, 1)


class Stage:

    def __init__(self, sem, per, unit=1):
        self.sem, self.per, self.unit = sem, per, unit

    def open(self, eng):
        eng.sem_inc(self.sem, self.per * self.unit)

    def now(self, eng, c, steps=None):
        steps = self.per if steps is None else steps
        eng.wait_ge(self.sem, c * (self.per * self.unit) + (self.per + steps) * self.unit)

    def before(self, eng, c, steps=None):
        steps = self.per if steps is None else steps
        eng.wait_ge(self.sem, c * (self.per * self.unit) + steps * self.unit)


def mixer_phase(nc, io, sc, y):
    with ExitStack() as ctx:
        def sb(name, shape, dt=F32):
            return ctx.enter_context(nc.sbuf_tensor(name, shape, dt))

        psum = ctx.enter_context(nc.psum_tensor("b_psum", [P, 8, 512], F32))
        cst = sb("b_cst", [P, C_W_ALL])
        gates = sb("b_gates", [P, NCH, 5 * GH])
        gc = sb("gates_chunk", [P, 4 * GH])
        qk_in = sb("qk_in", [P, 16, CH])
        v_in = sb("v_in", [P, 8, CH])
        z_in = sb("z_in", [P, 16, CH])
        r_in = sb("r_in", [P, 24, CH])
        qk = sb("qk_normed", [P, 16, CH])
        sq = sb("qk_squares", [P, 16, CH])
        rr = sb("qk_norms", [P, 16, CH])
        ug = sb("log_g_spread", [P, GH, CH])
        LOG_G, BETA, G_COL, BETA_EG, EG_LAST = (slice(n * GH, n * GH + GH) for n in range(5))
        dT = sb("decay_T", [P, GH, CH])
        dN = sb("decay_N", [P, GH, CH])
        eg = sb("exp_g_row", [P, GH, CH])
        M = sb("M", [P, GH, CH])
        attn = sb("attn_T", [P, GH, CH])
        XT = sb("XT", [P, GH, CH])
        X = sb("X", [P, GH, CH])
        Q = sb("Q", [P, GH, 64])
        vb = sb("v_beta", [P, GH, CH])
        kbg = sb("k_beta_exp_g", [P, GH, CH])
        kd = sb("k_decayed", [P, GH, CH])
        wT = sb("minus_w_T", [P, GH, CH])
        vnew = sb("v_new", [P, GH, CH])
        qd = sb("q_decayed", [P, GH, CH])
        S = sb("S", [P, GH, P])
        Sd = sb("S_decayed", [P, GH, P])
        osq = sb("o_squares", [P, 8, CH])
        ro = sb("o_norms", [P, GH, CH])
        oz = sb("o_gated", [P, GH, CH])
        rsc = sb("r_scores", [P, RH, CH])
        rkd = sb("r_k_decayed", [P, RH, 256])
        rv = sb("r_v", [P, RH, 256])
        rqd = sb("r_q_decayed", [P, 8, CH])
        rS = sb("r_S", [P, RH, 2, 256])
        rro = sb("r_o_norms", [P, RH, CH])
        roz = sb("r_o_gated", [P, 8, CH])

        stages = []

        def stage(name, per, unit=1):
            st = Stage(ctx.enter_context(nc.semaphore(name)), per, unit)
            stages.append(st)
            return st

        tables = ctx.enter_context(nc.semaphore("b_tables"))
        s_zero = ctx.enter_context(nc.semaphore("s_zero"))
        cumulated, g_cols = ctx.enter_context(nc.semaphore("cumulated")), ctx.enter_context(nc.semaphore("g_cols"))
        qk_load, v_load = stage("qk_load", 1, 16), stage("v_load", 1, 16)
        z_load, r_load = stage("z_load", 1, 16), stage("r_load", 1, 16)
        g_spread, s_dec, x_init, q_dec, r_qdec = (stage(n, k) for n, k in (
            ("g_spread", 2), ("s_dec", 1), ("x_init", 1), ("q_dec", 1), ("r_qdec", 1)))
        (pe_ss, pe_g, pe_rsc, pe_qk, pe_tr, pe_Q, pe_R, pe_T, pe_rtr, pe_ro, pe_rss, pe_rS, pe_w, pe_u, pe_o, pe_S,
         pe_oss) = (stage(n, k) for n, k in (
            ("pe_ss", 2), ("pe_g", 1), ("pe_rsc", 1), ("pe_qk", 4), ("pe_tr", 2), ("pe_Q", 14), ("pe_R", 12),
            ("pe_T", 12), ("pe_rtr", 2), ("pe_ro", 1), ("pe_rss", 1), ("pe_rS", 2), ("pe_w", 2), ("pe_u", 2),
            ("pe_o", 2), ("pe_S", 2), ("pe_oss", 2)))
        (a_sq, a_ln, a_norm, a_decay, a_eg, a_X, a_w, a_v, a_osq, a_oln, a_onorm, a_rv, a_rosq, a_roln,
         a_ronorm) = (stage(n, k) for n, k in (
            ("a_sq", 2), ("a_ln", 2), ("a_norm", 2), ("a_decay", 2), ("a_eg", 1), ("a_X", 12),
            ("a_w", 2), ("a_v", 2), ("a_osq", 2), ("a_oln", 1), ("a_onorm", 1), ("a_rv", 1), ("a_rosq", 1),
            ("a_roln", 1), ("a_ronorm", 1)))
        (d_diff, d_bounded, d_qk, d_attn, d_M, d_Q, d_XT, d_vb, d_kbg, d_kd, d_S, d_oz, d_y, d_rsc, d_rkd,
         d_rS, d_roz, d_ry, d_sum) = (stage(n, k) for n, k in (
            ("d_diff", 1), ("d_bounded", 2), ("d_qk", 2), ("d_attn", 4), ("d_M", 8), ("d_Q", 14),
            ("d_XT", 14), ("d_vb", 2), ("d_kbg", 2), ("d_kd", 2), ("d_S", 2), ("d_oz", 2), ("d_y", 1),
            ("d_rsc", 1), ("d_rkd", 1), ("d_rS", 4), ("d_roz", 1), ("d_ry", 1), ("d_sum", 1)))
        block = ctx.enter_context(nc.Block())

        def const(at, n):
            return cst[:, at:at + n]

        ident, ones = const(C_ID, P), const(C_ONES, P)
        eps, lnq = const(C_EPS, 1), const(C_LNQ, 1)

        def odd(x, g, lv):
            return x[:, 4 * g:4 * g + 4, :].rearrange("p h (n t b) -> p (h n) t b", t=2, b=1 << lv)[:, :, 1, :]

        def heads(g):
            return slice(4 * g, 4 * g + 4)

        def four(bank):
            return psum[:, bank, :].rearrange("p (h c) -> p h c", h=4)

        @block.sync
        def _(sp):
            sp.dma_start(cst[:, :], io["cst"]).then_inc(tables, 16)
            sp.dma_start(gates[:, :, 0:2 * GH], sc["gates"]).then_inc(tables, 16)
            for st in (qk_load, v_load, z_load, r_load):
                st.open(sp)
            mix = sc["mix"].rearrange("s p c -> p s c")
            with sp.Fori(0, NCH) as c:
                col = sp.snap(c * CH)

                def load(st, buf, first, n):
                    sp.dma_start(buf[:, :, :], mix[:, first:first + n, bass.ds(col, CH)]).then_inc(st.sem, 16)

                a_sq.before(sp, c)
                d_qk.before(sp, c)
                load(qk_load, qk_in, S_Q, 16)
                pe_tr.before(sp, c)
                load(v_load, v_in, S_V, 8)
                r_qdec.before(sp, c)
                pe_rsc.before(sp, c)
                pe_rtr.before(sp, c)
                load(r_load, r_in, S_RQ, 24)
                d_roz.before(sp, c)
                d_oz.before(sp, c)
                load(z_load, z_in, S_ZA, 16)

        @block.gpsimd
        def _(pool):
            for st in (g_spread, s_dec, x_init, q_dec, r_qdec):
                st.open(pool)
            pool.memset(S[:, :, :], 0.0).then_inc(s_zero, 1)
            pool.memset(rS[:, :, :, :], 0.0).then_inc(s_zero, 1)
            pool.wait_ge(tables, 32)

            def spread_g(c):
                pe_g.before(pool, c)
                d_M.before(pool, c)
                d_vb.before(pool, c)
                d_kbg.before(pool, c)
                d_diff.before(pool, c)
                pool.tensor_tensor(gc[:, :].rearrange("p (o g) -> p o g", o=1), gates[:, bass.ds(c, 1), 0:4 * GH],
                                   const(C_ONES, 4 * GH).rearrange("p (o g) -> p o g", o=1),
                                   ALU.mult).then_inc(g_spread.sem, 1)
                g_spread.now(pool, c, 1)
                pool.tensor_tensor(ug[:, :, :],
                                   const(C_TRIU, P).rearrange("p (o c) -> p o c", o=1).broadcast_to((P, GH, CH)),
                                   gc[:, 0:GH].rearrange("p (g o) -> p g o", o=1).broadcast_to((P, GH, CH)),
                                   ALU.mult).then_inc(g_spread.sem, 1)

            def decay_rq(c):
                r_load.now(pool, c)
                pe_ro.before(pool, c)
                rq = r_in[:, 0:8, :].rearrange("p (h a) c -> p h a c", a=2)
                row = const(C_RROW, RH * CH).rearrange("p (h o c) -> p h o c", h=RH, o=1)
                pool.tensor_tensor(rqd[:, :, :].rearrange("p (h a) c -> p h a c", a=2), rq,
                                   row.broadcast_to((P, RH, 2, CH)), ALU.mult).then_inc(r_qdec.sem, 1)

            def decay_s(c):
                d_S.before(pool, c)
                pool.tensor_tensor(Sd[:, :, :], S[:, :, :], gates[:, bass.ds(c, 1), EG_LAST].rearrange(
                    "p o g -> p g o").broadcast_to((P, GH, P)), ALU.mult).then_inc(s_dec.sem, 1)

            def start_x(c):
                def even(x):
                    return x.rearrange("p h (n t) -> p h n t", t=2)[:, :, :, 0]

                pe_u.before(pool, c)
                pool.tensor_tensor(even(XT[:, :, :]),
                                   even(ident.rearrange("p (o c) -> p o c", o=1).broadcast_to((P, GH, CH))),
                                   even(ones.rearrange("p (o c) -> p o c", o=1).broadcast_to((P, GH, CH))),
                                   ALU.mult).then_inc(x_init.sem, 1)

            def decay_q(c):
                a_eg.now(pool, c)
                d_qk.now(pool, c)
                pe_o.before(pool, c)
                pool.tensor_tensor(qd[:, :, :], qk[:, 0:8, :], eg[:, :, :], ALU.mult).then_inc(q_dec.sem, 1)

            def prepare(c):
                spread_g(c)
                decay_rq(c)
                start_x(c)
                decay_s(c)
                decay_q(c)

            pool.wait_ge(g_cols, 4)
            prepare(0)
            with pool.Fori(0, NCH - 1) as c:
                prepare(c + 1)

        @block.tensor
        def _(pe):
            for st in (pe_ss, pe_g, pe_rsc, pe_qk, pe_tr, pe_Q, pe_R, pe_T, pe_rtr, pe_ro, pe_rss, pe_rS, pe_w, pe_u,
                       pe_o, pe_S, pe_oss):
                st.open(pe)
            pe.wait_ge(tables, 32)
            pe.wait_ge(s_zero, 2)

            def sum_squares(c, half):
                a_sq.now(pe, c, half + 1)
                if half:
                    a_ln.now(pe, c, 1)
                else:
                    a_eg.now(pe, c)
                    d_diff.now(pe, c)
                for b in range(2):
                    n = 2 * half + b
                    mm = pe.matmul(psum[:, 2 + b, :], ones, sq[:, 4 * n:4 * n + 4, :], start=True, stop=True)
                mm.then_inc(pe_ss.sem, 1)

            def cumulate_g(c):
                g_spread.now(pe, c)
                a_rv.before(pe, c)
                for g in range(2):
                    mm = pe.matmul(psum[:, 2 + g, :], ones, ug[:, heads(g), :], start=True, stop=True)
                mm.then_inc(pe_g.sem, 1)

            def multiply_retention(c):
                a_ln.now(pe, c)
                r_load.now(pe, c)
                for h in range(RH):
                    for a in range(2):
                        mm = pe.matmul(psum[:, 2, h * CH:(h + 1) * CH], r_in[:, 8 + 2 * h + a, :],
                                       r_in[:, 2 * h + a, :], start=(a == 0), stop=(a == 1))
                mm.then_inc(pe_rsc.sem, 1)

            def multiply_qk(c):
                d_qk.now(pe, c)
                d_rS.before(pe, c)
                d_rsc.now(pe, c)
                pairs = qk[:, :, :].rearrange("p (w h) c -> p w h c", w=2)
                for h in range(GH):
                    mm = pe.matmul(psum[:, h // 2, (h % 2) * 256:(h % 2) * 256 + 256].rearrange(
                        "p (w c) -> p w c", w=2), qk[:, 8 + h, :], pairs[:, :, h, :], start=True, stop=True)
                    if h % 2:
                        mm.then_inc(pe_qk.sem, 1)

            def chunk(c, last=False):
                def turn_qkv():
                    v_load.now(pe, c)
                    d_attn.now(pe, c)
                    d_M.now(pe, c)
                    a_oln.before(pe, c)
                    for src, first, bank in ((v_in, 0, 0), (qk, 8, 2)):
                        for h in range(GH):
                            mm = pe.transpose(psum[:, bank + h // 4, (h % 4) * P:(h % 4) * P + P],
                                              src[:, first + h, :], ident)
                        mm.then_inc(pe_tr.sem, 1)

                def turn_retention():
                    d_vb.now(pe, c)
                    d_kbg.now(pe, c)
                    d_kd.now(pe, c)
                    for first, bank in ((8, 0), (16, 2)):
                        for t in range(8):
                            mm = pe.transpose(psum[:, bank + t // 4, (t % 4) * P:(t % 4) * P + P],
                                              r_in[:, first + t, :], ident)
                        mm.then_inc(pe_rtr.sem, 1)

                def retention_out():
                    d_rkd.now(pe, c)
                    a_rv.now(pe, c)
                    d_rsc.now(pe, c)
                    r_qdec.now(pe, c)
                    d_rS.before(pe, c)
                    for h in range(RH):
                        for e in range(2):
                            t = 2 * h + e
                            o = psum[:, t // 4, (t % 4) * CH:(t % 4) * CH + CH]
                            pe.matmul(o, rv[:, h, e * P:e * P + P], rsc[:, h, :], start=True, stop=False)
                            for a in range(2):
                                mm = pe.matmul(o, rS[:, h, a, e * P:e * P + P], rqd[:, 2 * h + a, :],
                                               start=False, stop=(a == 1))
                    mm.then_inc(pe_ro.sem, 1)

                def retention_norm():
                    a_rosq.now(pe, c)
                    d_roz.now(pe, c)
                    for h in range(RH):
                        for e in range(2):
                            mm = pe.matmul(psum[:, 0, h * CH:(h + 1) * CH], ones, osq[:, 2 * h + e, :],
                                           start=(e == 0), stop=(e == 1))
                    mm.then_inc(pe_rss.sem, 1)

                def retention_state(half):
                    if half:
                        d_rS.now(pe, c, 2)
                    else:
                        a_roln.now(pe, c)
                    for h in range(2 * half, 2 * half + 2):
                        for a in range(2):
                            mm = pe.matmul(psum[:, h % 2, a * 256:a * 256 + 256], rkd[:, h, a * P:a * P + P],
                                           rv[:, h, :], start=True, stop=True)
                    mm.then_inc(pe_rS.sem, 1)

                d_S.before(pe, c)
                inside = {0: turn_qkv, 1: turn_retention, 2: retention_out, 3: retention_norm,
                          4: lambda: retention_state(0), 5: lambda: retention_state(1)}
                after = {}
                if not last:
                    after = {2: lambda: cumulate_g(c + 1), 3: lambda: sum_squares(c + 1, 0),
                             4: lambda: sum_squares(c + 1, 1), 5: lambda: multiply_retention(c + 1)}
                for lv in range(NLEVEL):
                    for g in range(2):
                        if lv == 1:
                            x_init.now(pe, c)
                            d_oz.before(pe, c)
                        if lv:
                            d_XT.now(pe, c, 2 * lv - 1 + g)
                            for h in range(4):
                                mm = pe.transpose(psum[:, 6 + g, h * P:h * P + P], XT[:, 4 * g + h, :], ident)
                            mm.then_inc(pe_T.sem, 1)
                        d_M.now(pe, c, 4 * g + 4)
                        for h in range(4):
                            x = XT[:, 4 * g + h, :] if lv else ident
                            rhs = x.rearrange("p (n t b) -> p n t b", t=2, b=1 << lv)[:, :, 1, :]
                            out = psum[:, 4 + g, h * 64:h * 64 + 64].rearrange("p (n b) -> p n b", b=1 << lv)
                            mm = pe.matmul(out, M[:, 4 * g + h, :], rhs, start=True, stop=True)
                        mm.then_inc(pe_Q.sem, 1)
                    if lv in inside:
                        inside[lv]()
                    if lv:
                        for g in range(2):
                            a_X.now(pe, c, 2 * lv - 1 + g)
                            d_Q.now(pe, c, 2 * lv + 1 + g)
                            for h in range(4):
                                mm = pe.matmul(psum[:, 4 + g, 256 + h * 64:256 + h * 64 + 64], X[:, 4 * g + h, :],
                                               Q[:, 4 * g + h, :], start=True, stop=True)
                            mm.then_inc(pe_R.sem, 1)
                    if lv in after:
                        after[lv]()
                a_X.now(pe, c)
                d_kbg.now(pe, c)
                for g in range(2):
                    d_XT.now(pe, c, 13 + g)
                    for h in range(4):
                        mm = pe.matmul(psum[:, 6 + g, h * CH:(h + 1) * CH], kbg[:, 4 * g + h, :], XT[:, 4 * g + h, :],
                                       start=True, stop=True)
                    mm.then_inc(pe_w.sem, 1)
                if last:
                    d_rS.now(pe, c)
                else:
                    multiply_qk(c + 1)
                d_vb.now(pe, c)
                d_S.before(pe, c)
                for g in range(2):
                    a_w.now(pe, c, g + 1)
                    for h in range(4 * g, 4 * g + 4):
                        o = psum[:, 4 + g, (h % 4) * P:(h % 4) * P + P]
                        pe.matmul(o, XT[:, h, :], vb[:, h, :], start=True, stop=False)
                        mm = pe.matmul(o, wT[:, h, :], S[:, h, :], start=False, stop=True)
                    mm.then_inc(pe_u.sem, 1)
                q_dec.now(pe, c)
                for g in range(2):
                    a_v.now(pe, c, g + 1)
                    for h in range(4 * g, 4 * g + 4):
                        o = psum[:, 6 + g, (h % 4) * CH:(h % 4) * CH + CH]
                        pe.matmul(o, S[:, h, :], qd[:, h, :], start=True, stop=False)
                        mm = pe.matmul(o, vnew[:, h, :], attn[:, h, :], start=False, stop=True)
                    mm.then_inc(pe_o.sem, 1)
                for g in range(2):
                    for h in range(4 * g, 4 * g + 4):
                        mm = pe.matmul(psum[:, 4 + g, (h % 4) * P:(h % 4) * P + P], kd[:, h, :], vnew[:, h, :],
                                       start=True, stop=True)
                    mm.then_inc(pe_S.sem, 1)
                if not last:
                    d_M.now(pe, c + 1)
                    d_attn.now(pe, c + 1)
                for g in range(2):
                    a_osq.now(pe, c, g + 1)
                    pe.matmul(psum[:, g, :], ones, osq[:, heads(g), :], start=True, stop=True).then_inc(pe_oss.sem, 1)

            pe.matmul(psum[:, 0, 0:NCH * GH], const(C_TRIU, P), gates[:, :, LOG_G], start=True, stop=True)
            pe.matmul(psum[:, 1, 0:NCH * GH], ones, gates[:, :, LOG_G], start=True, stop=True).then_inc(cumulated, 1)
            cumulate_g(0)
            sum_squares(0, 0)
            sum_squares(0, 1)
            multiply_retention(0)
            pe.wait_ge(g_cols, 4)
            multiply_qk(0)
            with pe.Fori(0, NCH - 1) as c:
                chunk(c)
            chunk(NCH - 1, last=True)

        @block.scalar
        def _(act):
            for st in (a_sq, a_ln, a_norm, a_decay, a_eg, a_X, a_w, a_v, a_osq, a_oln, a_onorm, a_rv, a_rosq,
                       a_roln, a_ronorm):
                st.open(act)
            act.preload_act_table_set("natural_log_exp_and_others")
            act.wait_ge(tables, 32)

            def square_qk(c):
                qk_load.now(act, c)
                pe_ss.before(act, c)
                for half in range(2):
                    w = slice(8 * half, 8 * half + 8)
                    act.activation(sq[:, w, :], qk_in[:, w, :], ACT.Square).then_inc(a_sq.sem, 1)

            def norm_qk(c, half):
                d_qk.before(act, c)
                w = slice(8 * half, 8 * half + 8)
                pe_ss.now(act, c, half + 1)
                act.activation(rr[:, w, :].rearrange("p (b h) c -> p b (h c)", b=2), psum[:, 2:4, :], ACT.Ln,
                               bias=eps).then_inc(a_ln.sem, 1)
                a_ln.now(act, c, half + 1)
                act.activation(rr[:, w, :], rr[:, w, :], ACT.Exp, scale=-0.5,
                               bias=0.0 if half else lnq).then_inc(a_norm.sem, 1)

            def rows_g(c):
                d_diff.now(act, c)
                q_dec.before(act, c)
                act.activation(eg[:, :, :].rearrange("p (b h) c -> p b (h c)", b=2), psum[:, 2:4, :],
                               ACT.Exp).then_inc(a_eg.sem, 1)

            def decays(c):
                d_bounded.now(act, c)
                act.activation(dN[:, :, :], dN[:, :, :], ACT.Exp, scale=-1.0).then_inc(a_decay.sem, 1)
                act.activation(dT[:, :, :], dT[:, :, :], ACT.Exp).then_inc(a_decay.sem, 1)

            def chunk(c, last=False):
                def retention_v():
                    pe_rtr.now(act, c, 2)
                    pe_rS.before(act, c)
                    pe_ro.before(act, c)
                    act.activation(rv[:, :, :].rearrange("p (b h) c -> p b (h c)", b=2), psum[:, 2:4, :],
                                   ACT.Copy).then_inc(a_rv.sem, 1)

                def retention_squares():
                    pe_ro.now(act, c)
                    pe_oss.before(act, c)
                    act.activation(osq[:, :, :].rearrange("p (b h) c -> p b (h c)", b=2), psum[:, 0:2, :],
                                   ACT.Square).then_inc(a_rosq.sem, 1)

                def retention_norms():
                    pe_rss.now(act, c)
                    d_ry.before(act, c)
                    act.activation(rro[:, :, :], four(0), ACT.Ln, bias=eps, scale=1.0 / 256).then_inc(a_roln.sem, 1)
                    a_roln.now(act, c)
                    act.activation(rro[:, :, :], rro[:, :, :], ACT.Exp, scale=-0.5).then_inc(a_ronorm.sem, 1)

                fill = {1: [retention_v], 2: [retention_squares], 3: [], 4: [], 5: [], 6: []}
                if not last:
                    fill[1].append(lambda: square_qk(c + 1))
                    fill[3].append(lambda: rows_g(c + 1))
                    fill[4].append(lambda: norm_qk(c + 1, 0))
                    fill[5].append(lambda: norm_qk(c + 1, 1))
                    fill[6].append(lambda: decays(c + 1))
                fill[3].append(retention_norms)
                for lv in range(1, NLEVEL):
                    for g in range(2):
                        pe_T.now(act, c, 2 * lv - 1 + g)
                        if lv > 1:
                            pe_R.now(act, c, 2 * lv - 3 + g)
                        else:
                            pe_R.before(act, c)
                        act.activation(X[:, heads(g), :], four(6 + g), ACT.Copy).then_inc(a_X.sem, 1)
                    for piece in fill[lv]:
                        piece()
                for g in range(2):
                    pe_w.now(act, c, g + 1)
                    pe_u.before(act, c)
                    act.activation(wT[:, heads(g), :], four(6 + g), ACT.Copy, scale=-1.0).then_inc(a_w.sem, 1)
                for g in range(2):
                    pe_u.now(act, c, g + 1)
                    pe_o.before(act, c)
                    pe_S.before(act, c)
                    act.activation(vnew[:, heads(g), :], four(4 + g), ACT.Copy).then_inc(a_v.sem, 1)
                for g in range(2):
                    pe_o.now(act, c, g + 1)
                    pe_rss.now(act, c)
                    act.activation(osq[:, heads(g), :], four(6 + g), ACT.Square).then_inc(a_osq.sem, 1)
                pe_oss.now(act, c)
                d_y.before(act, c)
                act.activation(ro[:, :, :].rearrange("p (b h) c -> p b (h c)", b=2), psum[:, 0:2, :], ACT.Ln,
                               bias=eps, scale=1.0 / P).then_inc(a_oln.sem, 1)
                a_oln.now(act, c)
                act.activation(ro[:, :, :], ro[:, :, :], ACT.Exp, scale=-0.5).then_inc(a_onorm.sem, 1)

            act.wait_ge(g_cols, 1)
            act.activation(gates[:, :, BETA_EG], gates[:, :, G_COL], ACT.Exp).then_inc(g_cols, 1)
            act.activation(gates[:, :, EG_LAST], psum[:, 1, 0:NCH * GH].rearrange("p (c g) -> p c g", g=GH),
                           ACT.Exp).then_inc(g_cols, 1)
            square_qk(0)
            rows_g(0)
            norm_qk(0, 0)
            norm_qk(0, 1)
            decays(0)
            with act.Fori(0, NCH - 1) as c:
                chunk(c)
            chunk(NCH - 1, last=True)

        @block.vector
        def _(dve):
            for st in (d_diff, d_bounded, d_qk, d_attn, d_M, d_Q, d_XT, d_vb, d_kbg, d_kd, d_S, d_oz, d_y, d_rsc,
                       d_rkd, d_rS, d_roz, d_ry, d_sum):
                st.open(dve)
            dve.wait_ge(tables, 32)
            dve.wait_ge(s_zero, 2)

            def differences(c):
                pe_g.now(dve, c)
                g_spread.now(dve, c, 1)
                d_attn.before(dve, c)
                d_kd.before(dve, c)
                dve.tensor_tensor(dT[:, :, :], psum[:, 2:4, :].rearrange("p b (h c) -> p (b h) c", h=4),
                                  gc[:, 2 * GH:3 * GH].rearrange("p (g o) -> p g o", o=1).broadcast_to((P, GH, CH)),
                                  ALU.subtract).then_inc(d_diff.sem, 1)

            def bound(c, out, table, op):
                if out is dN:
                    d_diff.now(dve, c)
                    d_M.before(dve, c)
                else:
                    d_bounded.now(dve, c, 1)
                dve.tensor_tensor(out[:, :, :], dT[:, :, :],
                                  const(table, P).rearrange("p (o c) -> p o c", o=1).broadcast_to((P, GH, CH)),
                                  op).then_inc(d_bounded.sem, 1)

            def retention_scores(c):
                pe_rsc.now(dve, c)
                pe_ro.before(dve, c)
                dve.tensor_tensor(rsc[:, :, :], four(2), const(C_RDEC, RH * CH).rearrange(
                    "p (h c) -> p h c", h=RH), ALU.mult).then_inc(d_rsc.sem, 1)

            def norm_qk(c, half):
                pe_tr.before(dve, c)
                q_dec.before(dve, c)
                w = slice(8 * half, 8 * half + 8)
                a_norm.now(dve, c, half + 1)
                dve.tensor_tensor(qk[:, w, :], qk_in[:, w, :], rr[:, w, :], ALU.mult).then_inc(d_qk.sem, 1)

            def make_m(c):
                a_decay.now(dve, c, 1)
                pe_Q.before(dve, c)
                for h in range(GH):
                    if h % 2 == 0:
                        pe_qk.now(dve, c, h // 2 + 1)
                    dve.scalar_tensor_tensor(out=M[:, h, :], in0=four(h // 2)[:, 2 * (h % 2) + 1, :],
                                             scalar=gc[:, GH + h:GH + h + 1], in1=dN[:, h, :], op0=ALU.mult,
                                             op1=ALU.mult).then_inc(d_M.sem, 1)

            def make_attn(c):
                a_decay.now(dve, c, 2)
                pe_o.before(dve, c)
                for b in range(4):
                    dve.tensor_tensor(attn[:, 2 * b:2 * b + 2, :],
                                      four(b).rearrange("p (h w) c -> p h w c", w=2)[:, :, 0, :],
                                      dT[:, 2 * b:2 * b + 2, :], ALU.mult).then_inc(d_attn.sem, 1)

            def mask_q(c, lv, g):
                pe_Q.now(dve, c, 2 * lv + 1 + g)
                if lv > 1:
                    pe_R.now(dve, c, 2 * lv - 3 + g)
                elif lv == 0:
                    pe_R.before(dve, c)
                else:
                    d_XT.now(dve, c, g + 1)
                mask = const(C_LEVEL + 64 * lv, 64).rearrange("p (o c) -> p o c", o=1)
                dve.tensor_tensor(Q[:, heads(g), :], psum[:, 4 + g, 0:256].rearrange("p (h c) -> p h c", h=4),
                                  mask.broadcast_to((P, 4, 64)), ALU.mult).then_inc(d_Q.sem, 1)

            def first_level(c):
                pe_u.before(dve, c)
                for g in range(2):
                    mask_q(c, 0, g)
                for g in range(2):
                    d_Q.now(dve, c, g + 1)
                    dve.tensor_tensor(XT[:, heads(g), 1::2], Q[:, heads(g), :],
                                      const(C_ID, P)[:, 1::2].rearrange("p (o c) -> p o c", o=1).broadcast_to(
                                          (P, 4, 64)), ALU.add).then_inc(d_XT.sem, 1)

            def chunk(c, last=False):
                def spread(col):
                    return col.rearrange("p (h o) -> p h o", o=1).broadcast_to((P, 4, CH))

                def delta_kv():
                    pe_u.before(dve, c)
                    pe_w.before(dve, c)
                    pe_S.before(dve, c)
                    for g in range(2):
                        pe_tr.now(dve, c, 1)
                        dve.tensor_tensor(vb[:, heads(g), :], four(g), spread(gc[:, GH + 4 * g:GH + 4 * g + 4]),
                                          ALU.mult).then_inc(d_vb.sem, 1)
                    for g in range(2):
                        pe_tr.now(dve, c, 2)
                        dve.tensor_tensor(kbg[:, heads(g), :], four(2 + g), spread(gc[:, 3 * GH + 4 * g:3 * GH + 4 * g + 4]),
                                          ALU.mult).then_inc(d_kbg.sem, 1)
                        dve.tensor_tensor(kd[:, heads(g), :], four(2 + g),
                                          dT[:, heads(g), CH - 1:CH].broadcast_to((P, 4, CH)),
                                          ALU.mult).then_inc(d_kd.sem, 1)

                def retention_k():
                    pe_rtr.now(dve, c, 1)
                    pe_rS.before(dve, c)
                    col = const(C_RCOL, RH).rearrange("p (h o) -> p h o", o=1).broadcast_to((P, RH, 256))
                    dve.tensor_tensor(rkd[:, :, :], psum[:, 0:2, :].rearrange("p b (h c) -> p (b h) c", h=2), col,
                                      ALU.mult).then_inc(d_rkd.sem, 1)

                def retention_gate():
                    z_load.now(dve, c)
                    a_rosq.now(dve, c)
                    d_ry.before(dve, c)
                    dve.tensor_tensor(roz[:, :, :], psum[:, 0:2, :].rearrange("p b (h c) -> p (b h) c", h=4),
                                      z_in[:, 8:16, :], ALU.mult).then_inc(d_roz.sem, 1)

                def retention_y():
                    a_ronorm.now(dve, c)
                    d_roz.now(dve, c)
                    dve.tensor_tensor(roz[:, :, :].rearrange("p (h e) c -> p h e c", e=2),
                                      roz[:, :, :].rearrange("p (h e) c -> p h e c", e=2),
                                      rro[:, :, :].rearrange("p h (o c) -> p h o c", o=1).broadcast_to(
                                          (P, RH, 2, CH)), ALU.mult).then_inc(d_ry.sem, 1)

                def retention_state(half):
                    pe_rS.now(dve, c, half + 1)
                    for h in range(2 * half, 2 * half + 2):
                        keep = math.exp(CH * math.log(1.0 - 2.0 ** (-5.0 - h)))
                        s_all = rS[:, h, :, :].rearrange("p a e -> p (a e)")
                        dve.scalar_tensor_tensor(out=s_all, in0=s_all, scalar=keep, in1=psum[:, h % 2, :], op0=ALU.mult,
                                                 op1=ALU.add).then_inc(d_rS.sem, 1)

                inside = {1: [retention_k], 4: [], 6: []}
                after = {3: [], 2: [retention_gate], 4: [lambda: retention_state(0)], 5: [], 6: []}
                if not last:
                    after[2].append(lambda: differences(c + 1))
                    after[3].append(lambda: bound(c + 1, dN, C_BELOW, ALU.max))
                    inside[4].append(lambda: bound(c + 1, dT, C_UPTO, ALU.min))
                    after[5].append(lambda: norm_qk(c + 1, 0))
                    inside[6].append(lambda: norm_qk(c + 1, 1))
                    after[6].append(lambda: retention_scores(c + 1))
                after[5].append(lambda: retention_state(1))
                delta_kv()
                for lv in range(1, NLEVEL):
                    for g in range(2):
                        mask_q(c, lv, g)
                    for piece in inside.get(lv, ()):
                        piece()
                    for g in range(2):
                        pe_R.now(dve, c, 2 * lv - 1 + g)
                        more = psum[:, 4 + g, 256:512].rearrange("p (n b) -> p n b", b=1 << lv)
                        dve.tensor_tensor(odd(XT, g, lv), odd(XT, g, lv), more, ALU.add).then_inc(d_XT.sem, 1)
                    for piece in after.get(lv, ()):
                        piece()
                if not last:
                    make_m(c + 1)
                retention_y()
                if not last:
                    make_attn(c + 1)
                s_dec.now(dve, c)
                for g in range(2):
                    pe_S.now(dve, c, g + 1)
                    dve.tensor_tensor(S[:, heads(g), :], Sd[:, heads(g), :], four(4 + g), ALU.add).then_inc(d_S.sem, 1)
                d_sum.before(dve, c)
                for g in range(2):
                    a_osq.now(dve, c, g + 1)
                    dve.tensor_tensor(oz[:, heads(g), :], four(6 + g), z_in[:, heads(g), :],
                                      ALU.mult).then_inc(d_oz.sem, 1)
                if not last:
                    first_level(c + 1)
                a_onorm.now(dve, c)
                d_oz.now(dve, c)
                dve.tensor_tensor(oz[:, :, :], oz[:, :, :], ro[:, :, :], ALU.mult).then_inc(d_y.sem, 1)
                d_y.now(dve, c)
                d_ry.now(dve, c)
                dve.tensor_tensor(y[:, :, bass.ds(c * CH, CH)], oz[:, :, :], roz[:, :, :],
                                  ALU.add).then_inc(d_sum.sem, 1)

            dve.wait_ge(cumulated, 1)
            dve.tensor_copy(gates[:, :, G_COL], psum[:, 0, 0:NCH * GH].rearrange(
                "p (c g) -> p c g", g=GH)).then_inc(g_cols, 1)
            dve.wait_ge(g_cols, 3)
            dve.tensor_tensor(gates[:, :, BETA_EG], gates[:, :, BETA_EG], gates[:, :, BETA],
                              ALU.mult).then_inc(g_cols, 1)
            differences(0)
            bound(0, dN, C_BELOW, ALU.max)
            bound(0, dT, C_UPTO, ALU.min)
            norm_qk(0, 0)
            norm_qk(0, 1)
            retention_scores(0)
            make_m(0)
            make_attn(0)
            first_level(0)
            with dve.Fori(0, NCH - 1) as c:
                chunk(c)
            chunk(NCH - 1, last=True)


def output_phase(nc, io, sc, y, out):
    with ExitStack() as ctx:
        def sb(name, shape, dt=F32):
            return ctx.enter_context(nc.sbuf_tensor(name, shape, dt))

        def sem(name):
            return ctx.enter_context(nc.semaphore(name))

        psum = ctx.enter_context(nc.psum_tensor("c_psum", [P, 8, 512], F32))
        cst = sb("c_cst", [P, C_EPS + 1])
        par = sb("c_par", [P, PAR_W])
        gf = sb("norm_f_rows", [P, D])
        xh = sb("c_xh", [P, KC, C_W], F32R)
        xl = sb("c_xl", [P, KC, C_W], F32R)
        h = sb("residual_T", [P, KC, C_W])
        wraw = [sb(f"c_w_raw{s}", [P, KC, P]) for s in range(SLOTS)]
        wh = [sb(f"c_w_hi{s}", [P, KC, P], F32R) for s in range(SLOTS)]
        wl = [sb(f"c_w_lo{s}", [P, KC, P], F32R) for s in range(SLOTS)]
        draw = sb("down_raw", [P, D])
        dh = sb("down_hi", [P, D], F32R)
        dl = sb("down_lo", [P, D], F32R)
        ah = [sb(f"act_hi{s}", [P, SEQ], F32R) for s in range(SLOTS)]
        al = [sb(f"act_lo{s}", [P, SEQ], F32R) for s in range(SLOTS)]
        rsum = sb("row_sums", [P, 8])
        rln = sb("row_logs", [P, 8])
        rnorm = sb("row_norms", [P, 8])
        sq = [y[:, 0, 0:C_W], y[:, 1, 0:C_W]]
        ssq, rbc = y[:, 2, 0:C_W], y[:, 3, 0:C_W]
        xn = [y[:, 4, 0:C_W], y[:, 5, 0:C_W]]
        raw = [y[:, 6, 0:C_W], y[:, 7, 0:C_W]]
        acc = [y[:, 0, 0:SEQ], y[:, 1, 0:SEQ]]
        junk = [y[:, 2, 0:D], y[:, 3, 0:D]]
        rows = [y[:, 4, 0:D], y[:, 5, 0:D]]

        tables, h_in = sem("c_tables"), sem("h_in")
        w_loaded = [sem(f"c_w_loaded{s}") for s in range(SLOTS)]
        (w_hi, w_lo, mm_done, y_hi, y_split, h_added, squared, summed, ss_ready, ln_done, rms_ready, normed, x_hi,
         x_split, evac) = (sem("c_" + n) for n in (
            "w_hi", "w_lo", "mm_done", "y_hi", "y_split", "h_added", "squared", "summed", "ss_ready", "ln_done",
            "rms_ready", "normed", "x_hi", "x_split", "evac"))
        d_loaded, d_hi, d_lo = sem("down_loaded"), sem("down_hi_done"), sem("down_lo_done")
        conv, silu, prod, act_hi, act_lo = (sem("f_" + n) for n in ("conv", "silu", "prod", "act_hi", "act_lo"))
        down, added = sem("f_down"), sem("f_added")
        turned, row_sum, row_ln, row_norm, row_out = (sem("o_" + n) for n in ("turned", "sum", "ln", "norm", "out"))
        row_stored = [sem(f"o_stored{s}") for s in range(SLOTS)]
        block = ctx.enter_context(nc.Block())

        w_out = io["w_out"][0].rearrange("(k p) n -> p k n", p=P)
        w_up = io["w_ffn_up"][0].rearrange("(k p) n -> p k n", p=P)
        w_down = io["w_ffn_down"][0]
        ident, ones = cst[:, C_ID:C_ID + P], cst[:, C_ONES:C_ONES + P]
        eps = cst[:, C_EPS:C_EPS + 1]
        HALVES = 2 * KC
        ADD_BANKS = (6, 7, 0, 1, 2)

        def thirds(x):
            return x.rearrange("p (b c) -> p b c", b=3)

        @block.sync
        def _(sp):
            for s in range(SLOTS):
                sp.dma_start(wraw[s][:, :, :], w_out[:, :, P * s:P * s + P]).then_inc(w_loaded[s], 16)
            sp.dma_start(cst[:, :], io["cst"][:, 0:C_EPS + 1]).then_inc(tables, 16)
            sp.dma_start(par[:, :], sc["par"]).then_inc(tables, 16)
            sp.dma_start(h[:, :, :], sc["hT"][:, :, C_COL:T]).then_inc(h_in, 16)
            sp.dma_start(gf[:, :], io["norm_f"].rearrange("(o d) -> o d", o=1).broadcast_to((P, D))).then_inc(tables, 16)
            sp.dma_start(draw[:, :], w_down[0:P, :]).then_inc(d_loaded, 16)
            for m in range(2, KC):
                sp.wait_ge(w_lo, m - 1)
                sp.dma_start(wraw[m % 2][:, :, :], w_out[:, :, P * m:P * m + P]).then_inc(w_loaded[m % 2], 16)
            for s, col in ((0, 0), (1, D_FF)):
                sp.wait_ge(w_lo, KC - 1 + s)
                sp.dma_start(wraw[s][:, :, :], w_up[:, :, col:col + P]).then_inc(w_loaded[s], 16)

            def load(j):
                a_col, b_col, d_row = sp.snap(j * P), sp.snap(j * P + D_FF), sp.snap(j * P)
                for s, col in ((0, a_col), (1, b_col)):
                    sp.wait_ge(w_lo, j * 2 + (KC - 1 + s))
                    sp.dma_start(wraw[s][:, :, :], w_up[:, :, bass.ds(col, P)]).then_inc(w_loaded[s], 16)
                sp.wait_ge(d_lo, j)
                sp.dma_start(draw[:, :], w_down[bass.ds(d_row, P), :]).then_inc(d_loaded, 16)

            with sp.Fori(1, FT) as j:
                load(j)
            for t in range(SEQ // P):
                sp.wait_ge(row_out, t + 1)
                sp.dma_start(out[0, t * P:t * P + P, :], rows[t % 2]).then_inc(row_stored[t % 2], 16)
            for s in range(SLOTS):
                sp.wait_ge(row_stored[s], 16 * (SEQ // P // 2))

        @block.tensor
        def _(pe):
            for m in range(KC):
                pe.wait_ge(w_lo, m + 1)
                if m >= 2:
                    pe.wait_ge(h_added, m - 1)
                project(pe, psum, 3 * (m % 2), wh[m % 2], wl[m % 2], xh, xl, 0, C_N,
                        y_split if m == 0 else None).then_inc(mm_done, 1)
            pe.wait_ge(tables, 48)
            pe.wait_ge(summed, KC)
            for b in range(3):
                mm = pe.matmul(psum[:, 5 + b, 0:C_N], ones, ssq[:, b * C_N:(b + 1) * C_N], start=True, stop=True)
            mm.then_inc(ss_ready, 1)

            def up(j, s):
                pe.wait_ge(w_lo, j * 2 + (KC + s + 1))
                pe.wait_ge(evac, j * 2 + (s - 1))
                if s == 0:
                    pe.wait_ge(added, (j - 1) * HALVES)
                project(pe, psum, 3 * s, wh[s], wl[s], xh, xl, 0, C_N).then_inc(mm_done, 1)

            def down_product(j, s, first=False, last=False):
                pe.wait_ge(act_lo, j + 1)
                pe.wait_ge(d_lo, j + 1)
                if not last:
                    pe.wait_ge(evac, j * 2 + 3)
                for n in range(HALVES):
                    bank = ADD_BANKS[n % 5]
                    if n >= 5:
                        pe.wait_ge(added, j * HALVES + (n - 4))
                    elif not first:
                        pe.wait_ge(added, j * HALVES)
                    m, half = n // 2, slice((n % 2) * 512, (n % 2) * 512 + 512)
                    for part, (w, x) in enumerate(((dh, ah[s]), (dh, al[s]), (dl, ah[s]))):
                        mm = pe.matmul(psum[:, bank, :], w[:, m * P:m * P + P], x[:, half],
                                       start=(part == 0), stop=(part == 2))
                    mm.then_inc(down, 1)

            pe.wait_ge(rms_ready, 1)
            pe.wait_ge(h_added, KC)
            pe.wait_ge(w_lo, KC + 2)
            project_two(pe, psum, wh, wl, xh, xl, 0, C_N, x_split, mm_done)
            pe.wait_ge(w_lo, KC + 3)
            pe.wait_ge(evac, 1)
            project(pe, psum, 0, wh[0], wl[0], xh, xl, 0, C_N).then_inc(mm_done, 1)
            up(1, 1)
            down_product(0, 0, True)
            with pe.Fori(1, FT // 2) as i:
                for j, s in ((i * 2, 0), (i * 2 + 1, 1)):
                    up(j, 0)
                    up(j, 1)
                    down_product(j - 1, 1 - s)
            down_product(FT - 1, 1, last=True)
            for t in range(SEQ // P):
                pe.wait_ge(added, FT * HALVES)
                if t >= 4:
                    pe.wait_ge(row_out, t - 3)
                for m in range(KC):
                    mm = pe.transpose(psum[:, 2 * (t % 4) + m // 4, (m % 4) * P:(m % 4) * P + P],
                                      h[:, m, 2 + t * P:2 + t * P + P], ident)
                mm.then_inc(turned, 1)

        @block.scalar
        def _(act):
            act.preload_act_table_set("natural_log_exp_and_others")

            def split_high(n, s):
                act.wait_ge(w_loaded[s], n * 16)
                act.activation(wh[s][:, :, :], wraw[s][:, :, :], ACT.Copy).then_inc(w_hi, 1)

            def y_high(k):
                act.activation(xh[:, k, :], y[:, k, C_COL:T], ACT.Copy).then_inc(y_hi, 1)

            split_high(1, 0)
            y_high(0)
            split_high(1, 1)
            for k in range(1, KC):
                y_high(k)
            for m in range(KC):
                act.wait_ge(mm_done, m + 1)
                split_high(m // 2 + 2, m % 2)
                act.wait_ge(h_added, m + 1)
                act.wait_ge(y_split, KC)
                if m >= 2:
                    act.wait_ge(summed, m - 1)
                o = ssq if m == 0 else sq[m % 2]
                act.activation(o, h[:, m, :], ACT.Square).then_inc(squared, 1)
            act.wait_ge(tables, 48)
            act.wait_ge(ss_ready, 1)
            act.activation(thirds(rbc), psum[:, 5:8, 0:C_N], ACT.Ln, bias=eps, scale=1.0 / D).then_inc(ln_done, 1)
            act.wait_ge(ln_done, 1)
            act.activation(rbc, rbc, ACT.Exp, scale=-0.5).then_inc(rms_ready, 1)
            for k in range(KC):
                act.wait_ge(normed, k + 1)
                act.activation(xh[:, k, :], xn[k % 2], ACT.Copy).then_inc(x_hi, 1)
            act.preload_act_table_set("silu_and_others")

            def down_high(j, first):
                if not first:
                    act.wait_ge(down, j * HALVES)
                act.wait_ge(d_loaded, j * 16 + 16)
                act.activation(dh[:, :], draw[:, :], ACT.Copy).then_inc(d_hi, 1)

            def hidden(j, s, first=False, last=False):
                for half in range(2):
                    act.wait_ge(mm_done, j * 2 + (KC + 1 + half))
                    if not first:
                        act.wait_ge(conv, j * 6 - 3 + 3 * half)
                    act.activation(thirds(raw[half]), psum[:, 3 * half:3 * half + 3, 0:C_N],
                                   ACT.Copy).then_inc(evac, 1)
                    if not last:
                        split_high(j + (KC // 2 + 2), half)
                act.wait_ge(conv, j * 6 + 3)
                act.activation(acc[0], acc[0], ACT.Silu).then_inc(silu, 1)
                if not last:
                    down_high(j, first)
                act.wait_ge(prod, j + 1)
                act.activation(ah[s][:, :], acc[0], ACT.Copy).then_inc(act_hi, 1)
                if last:
                    down_high(j, first)

            hidden(0, 0, first=True)
            hidden(1, 1)
            with act.Fori(1, FT // 2 - 1) as i:
                hidden(i * 2, 0)
                hidden(i * 2 + 1, 1)
            hidden(FT - 2, 0)
            hidden(FT - 1, 1, last=True)
            act.preload_act_table_set("natural_log_exp_and_others")
            for t in range(SEQ // P):
                act.wait_ge(turned, t + 1)
                if t >= 2:
                    act.wait_ge(row_sum, t - 1)
                else:
                    act.wait_ge(prod, FT)
                act.activation(junk[t % 2].rearrange("p (b c) -> p b c", b=2),
                               psum[:, 2 * (t % 4):2 * (t % 4) + 2, :], ACT.Square,
                               accum_out=rsum[:, t:t + 1]).then_inc(row_sum, 1)
                act.wait_ge(row_sum, t + 1)
                act.activation(rln[:, t:t + 1], rsum[:, t:t + 1], ACT.Ln, bias=eps, scale=1.0 / D).then_inc(row_ln, 1)
                act.wait_ge(row_ln, t + 1)
                act.activation(rnorm[:, t:t + 1], rln[:, t:t + 1], ACT.Exp, scale=-0.5).then_inc(row_norm, 1)

        @block.vector
        def _(dve):
            def split_low(count, s):
                dve.wait_ge(w_hi, count)
                dve.tensor_tensor(wl[s][:, :, :], wraw[s][:, :, :], wh[s][:, :, :].bitcast(F32),
                                  ALU.subtract).then_inc(w_lo, 1)

            def y_low(k):
                dve.wait_ge(y_hi, k + 1)
                dve.tensor_tensor(xl[:, k, :], y[:, k, C_COL:T], xh[:, k, :].bitcast(F32),
                                  ALU.subtract).then_inc(y_split, 1)

            split_low(1, 0)
            y_low(0)
            split_low(2, 1)
            for k in range(1, KC):
                y_low(k)
            dve.wait_ge(h_in, 16)

            def add_square(m):
                if m:
                    dve.wait_ge(squared, m + 1)
                    dve.wait_ge(summed, m)
                    dve.tensor_tensor(ssq, ssq, sq[m % 2], ALU.add).then_inc(summed, 1)
                else:
                    dve.wait_ge(squared, 1)
                    dve.memset(rsum[:, :], 0.0).then_inc(summed, 1)

            for m in range(KC):
                dve.wait_ge(mm_done, m + 1)
                dve.tensor_tensor(thirds(h[:, m, :]), psum[:, 3 * (m % 2):3 * (m % 2) + 3, 0:C_N],
                                  thirds(h[:, m, :]), ALU.add).then_inc(h_added, 1)
                split_low(m + 3, m % 2)
                if m:
                    add_square(m - 1)
            add_square(KC - 1)
            dve.wait_ge(rms_ready, 1)
            dve.wait_ge(tables, 48)

            def low_part(k):
                dve.wait_ge(normed, k + 1)
                dve.wait_ge(x_hi, k + 1)
                dve.tensor_tensor(xl[:, k, :], xn[k % 2], xh[:, k, :].bitcast(F32), ALU.subtract).then_inc(x_split, 1)

            for k in range(KC):
                if k >= 2:
                    dve.wait_ge(x_split, k - 1)
                dve.scalar_tensor_tensor(out=xn[k % 2], in0=h[:, k, :], scalar=par[:, PAR_N2 + k:PAR_N2 + k + 1],
                                         in1=rbc, op0=ALU.mult, op1=ALU.mult).then_inc(normed, 1)
                if k:
                    low_part(k - 1)
            low_part(KC - 1)

            def taps(j, half):
                def weight(at):
                    return par[:, bass.ds(j + (at + FT * half), 1)]

                dve.wait_ge(evac, j * 2 + (half + 1))
                dve.tensor_scalar(acc[half], raw[half][:, 0:SEQ], weight(PAR_FCONV), weight(PAR_FB), ALU.mult,
                                  ALU.add).then_inc(conv, 1)
                for k in range(1, FCONV):
                    dve.wait_ge(conv, j * 6 + (3 * half + k))
                    dve.scalar_tensor_tensor(out=acc[half], in0=raw[half][:, k:k + SEQ],
                                             scalar=weight(PAR_FCONV + 2 * FT * k), in1=acc[half], op0=ALU.mult,
                                             op1=ALU.add).then_inc(conv, 1)

            def add_down(j, first=False):
                for n in range(HALVES):
                    at = h[:, n // 2, 2 + (n % 2) * 512:2 + (n % 2) * 512 + 512]
                    dve.wait_ge(down, j * HALVES + (n + 1))
                    if n == 0 and not first:
                        dve.wait_ge(added, j * HALVES)
                    dve.tensor_tensor(at, psum[:, ADD_BANKS[n % 5], :], at, ALU.add).then_inc(added, 1)

            def gate_product(j):
                dve.wait_ge(silu, j + 1)
                dve.wait_ge(conv, j * 6 + 6)
                dve.tensor_tensor(acc[0], acc[0], acc[1], ALU.mult).then_inc(prod, 1)

            def split_down(j):
                dve.wait_ge(d_hi, j + 1)
                dve.tensor_tensor(dl[:, :], draw[:, :], dh[:, :].bitcast(F32), ALU.subtract).then_inc(d_lo, 1)

            def split_act(j, s):
                dve.wait_ge(act_hi, j + 1)
                dve.tensor_tensor(al[s][:, :], acc[0], ah[s][:, :].bitcast(F32), ALU.subtract).then_inc(act_lo, 1)

            def hidden(j, s, first=False):
                if not first:
                    dve.wait_ge(act_lo, j)
                if first:
                    split_low(j * 2 + (KC + 3), 0)
                    split_low(j * 2 + (KC + 4), 1)
                taps(j, 0)
                if not first:
                    split_low(j * 2 + (KC + 3), 0)
                    add_down(j - 1, isinstance(j, int) and j == 1)
                taps(j, 1)
                if not first:
                    split_low(j * 2 + (KC + 4), 1)
                gate_product(j)
                split_down(j)
                split_act(j, s)

            def last_hidden(j, s):
                dve.wait_ge(act_lo, j)
                taps(j, 0)
                taps(j, 1)
                gate_product(j)
                add_down(j - 1)
                split_act(j, s)
                split_down(j)

            hidden(0, 0, first=True)
            hidden(1, 1)
            with dve.Fori(1, FT // 2 - 1) as i:
                hidden(i * 2, 0)
                hidden(i * 2 + 1, 1)
            hidden(FT - 2, 0)
            last_hidden(FT - 1, 1)
            add_down(FT - 1)
            for t in range(SEQ // P):
                dve.wait_ge(row_norm, t + 1)
                if t >= 2:
                    dve.wait_ge(row_stored[t % 2], 16 * (t // 2))
                dve.scalar_tensor_tensor(out=rows[t % 2].rearrange("p (b c) -> p b c", b=2),
                                         in0=psum[:, 2 * (t % 4):2 * (t % 4) + 2, :], scalar=rnorm[:, t:t + 1],
                                         in1=gf[:, :].rearrange("p (b c) -> p b c", b=2), op0=ALU.mult,
                                         op1=ALU.mult).then_inc(row_out, 1)


INPUTS = ("x", "meta", "norm1", "w_in", "gdn_conv_w", "gdn_a_log", "gdn_dt_bias", "gdn_norm", "w_out", "norm2",
          "w_ffn_up", "ffn_conv_w", "ffn_conv_b", "w_ffn_down", "norm_f")


def layer(nc, io, out):
    sc = {
        "mix": nc.dram_tensor("mix_scratch", (S_N, P, T), F32, kind="Internal").ap(),
        "hT": nc.dram_tensor("hT_scratch", (P, KC, T), F32, kind="Internal").ap(),
        "gates": nc.dram_tensor("gates_scratch", (P, NCH, 2 * GH), F32, kind="Internal").ap(),
        "par": nc.dram_tensor("par_scratch", (P, PAR_W), F32, kind="Internal").ap(),
    }
    input_phase(nc, io, sc)
    with nc.sbuf_tensor("y", [P, KC, T], F32) as y:
        mixer_phase(nc, io, sc, y)
        output_phase(nc, io, sc, y, out)


def kernel(**inputs):
    import concourse.bacc as _bacc
    from concourse.bass_utils import run_bass_kernel_spmd as _run

    nc = _bacc.Bacc("TRN2", target_bir_lowering=False, num_devices=1)
    consts, rope = shape_constants()
    arrays = {f"in_{n}": np.ascontiguousarray(inputs[n]) for n in INPUTS}
    arrays["in_cst"], arrays["in_rope"] = consts, np.ascontiguousarray(rope)
    io = {n[3:]: nc.dram_tensor(n, a.shape, mybir.dt.from_np(a.dtype), kind="ExternalInput").ap()
          for n, a in arrays.items()}
    out = nc.dram_tensor("out_0", (1, SEQ, D), F32, kind="ExternalOutput").ap()
    layer(nc, io, out)
    r = _run(nc, [arrays], core_ids=[0])
    return r.results[0]["out_0"]
```
